# Optimizing a Trainium2 kernel written in Bass

```python
import jax, jax.numpy as jnp
from jax import lax
import numpy as np

D_MODEL = 2048
BATCH = 1
SEQ = 256
DEPTH = 2

CHUNK = 64
MIX_WIDTH = D_MODEL
CONV_WIDTH = MIX_WIDTH // 2
ATTN_WIDTH = MIX_WIDTH - CONV_WIDTH
HEAD_DIM = 64
N_Q_HEADS = ATTN_WIDTH // HEAD_DIM
N_KV_HEADS = max(1, N_Q_HEADS // 8)
Q_PER_KV = N_Q_HEADS // N_KV_HEADS
KV_WIDTH = N_KV_HEADS * HEAD_DIM
CONV_K = 3
WINDOW = 128
WINDOW_CHUNKS = WINDOW // CHUNK
ROPE_THETA = 500000.0
ROPE_DIM = HEAD_DIM // 4
EPS = 1e-5
NEG_INF = -1e30
IN_SIZES = (CONV_WIDTH, CONV_WIDTH, CONV_WIDTH, CONV_WIDTH,
            ATTN_WIDTH, KV_WIDTH, KV_WIDTH, ATTN_WIDTH)
IN_COLS = sum(IN_SIZES)
IN_OFFSETS = tuple(int(o) for o in np.cumsum(IN_SIZES)[:-1])

kernel_name = "hybrid_shortconv_swa_sink_parallel_heads"

def rmsnorm(x, g):
    xf = x.astype(jnp.float32)
    xf = xf * lax.rsqrt(jnp.mean(xf * xf, axis=-1, keepdims=True) + EPS)
    return (xf * g.astype(jnp.float32)).astype(x.dtype)

def partial_rope(t, pos):
    half = ROPE_DIM // 2
    inv_freq = ROPE_THETA ** (-jnp.arange(half, dtype=jnp.float32) * 2.0 / ROPE_DIM)
    ang = pos.astype(jnp.float32)[:, None] * inv_freq[None, :]
    cos = jnp.cos(ang)[None, :, None, :]
    sin = jnp.sin(ang)[None, :, None, :]
    tf = t.astype(jnp.float32)
    t1, t2, rest = tf[..., :half], tf[..., half:ROPE_DIM], tf[..., ROPE_DIM:]
    out = jnp.concatenate([t1 * cos - t2 * sin, t2 * cos + t1 * sin, rest], axis=-1)
    return out.astype(t.dtype)

def short_conv_mixer(b_gate, c_gate, u, conv_w):
    h = c_gate * u
    s = h.shape[1]
    hp = jnp.pad(h, ((0, 0), (CONV_K - 1, 0), (0, 0)))
    y = hp[:, 0:s] * conv_w[0]
    for j in range(1, CONV_K):
        y = y + hp[:, j:j + s] * conv_w[j]
    return b_gate * y

def sliding_window_sink_attention(q, k, v, sinks):
    b, s = q.shape[0], q.shape[1]
    nc = s // CHUNK
    band_len = WINDOW_CHUNKS * CHUNK
    qc = q.reshape(b, nc, CHUNK, N_KV_HEADS, Q_PER_KV, HEAD_DIM)

    def band(t):
        tc = t.reshape(b, nc, CHUNK, N_KV_HEADS, HEAD_DIM)
        tp = jnp.pad(tc, ((0, 0), (WINDOW_CHUNKS - 1, 0), (0, 0), (0, 0), (0, 0)))
        return jnp.concatenate([tp[:, j:j + nc] for j in range(WINDOW_CHUNKS)], axis=2)

    kb, vb = band(k), band(v)
    logits = jnp.einsum('bcqkgd,bcskd->bckgqs', qc, kb).astype(jnp.float32) * (HEAD_DIM ** -0.5)
    key_chunk = (jnp.arange(nc)[:, None] - (WINDOW_CHUNKS - 1)
                 + (jnp.arange(band_len) // CHUNK)[None, :])
    valid = (key_chunk >= 0)[None, :, None, None, None, :]
    logits = jnp.where(valid, logits, NEG_INF)
    sink = sinks.astype(jnp.float32).reshape(N_KV_HEADS, Q_PER_KV)[None, None, :, :, None, None]
    m = jnp.maximum(jnp.max(logits, axis=-1, keepdims=True), sink)
    p = jnp.exp(logits - m)
    denom = jnp.sum(p, axis=-1, keepdims=True) + jnp.exp(sink - m)
    probs = (p / denom).astype(v.dtype)
    out = jnp.einsum('bckgqs,bcskd->bcqkgd', probs, vb)
    return out.reshape(b, s, ATTN_WIDTH)

def setup_inputs(seed: int = 0) -> dict:
    key = jax.random.key(seed)
    ks = jax.random.split(key, 10)
    f32 = jnp.float32
    x = jax.random.normal(ks[0], (BATCH, SEQ, D_MODEL), f32)
    norm_g = 1.0 + 0.02 * jax.random.normal(ks[1], (DEPTH, D_MODEL), f32)
    w_in = jax.random.normal(ks[2], (DEPTH, D_MODEL, IN_COLS), f32) * (D_MODEL ** -0.5)
    conv_w = jax.random.normal(ks[3], (DEPTH, CONV_K, CONV_WIDTH), f32) * (CONV_K ** -0.5)
    sinks = jax.random.normal(ks[4], (DEPTH, N_Q_HEADS), f32)
    gn_conv = 1.0 + 0.02 * jax.random.normal(ks[5], (DEPTH, CONV_WIDTH), f32)
    gn_attn = 1.0 + 0.02 * jax.random.normal(ks[6], (DEPTH, ATTN_WIDTH), f32)
    w_out = jax.random.normal(ks[7], (DEPTH, MIX_WIDTH, D_MODEL), f32) * (MIX_WIDTH ** -0.5)
    final_g = 1.0 + 0.02 * jax.random.normal(ks[8], (D_MODEL,), f32)
    return {"x": x, "norm_g": norm_g, "w_in": w_in, "conv_w": conv_w, "sinks": sinks,
            "gn_conv": gn_conv, "gn_attn": gn_attn, "w_out": w_out, "final_g": final_g}

def reference(x, norm_g, w_in, conv_w, sinks, gn_conv, gn_attn, w_out, final_g):
    b, s, _ = x.shape
    pos = jnp.arange(s, dtype=jnp.int32)
    for l in range(DEPTH):
        h = rmsnorm(x, norm_g[l])
        proj = jnp.einsum('bsd,dc->bsc', h, w_in[l])
        b_g, c_g, u, z_conv, q, k, v, z_attn = jnp.split(proj, IN_OFFSETS, axis=-1)
        y_conv = short_conv_mixer(b_g, c_g, u, conv_w[l])
        y_conv = rmsnorm(y_conv, gn_conv[l]) * jax.nn.silu(z_conv)
        q = partial_rope(q.reshape(b, s, N_Q_HEADS, HEAD_DIM), pos)
        k = partial_rope(k.reshape(b, s, N_KV_HEADS, HEAD_DIM), pos)
        v = v.reshape(b, s, N_KV_HEADS, HEAD_DIM)
        y_attn = sliding_window_sink_attention(q, k, v, sinks[l])
        y_attn = rmsnorm(y_attn, gn_attn[l]) * jax.nn.silu(z_attn)
        y = jnp.concatenate([y_conv, y_attn], axis=-1)
        x = x + jnp.einsum('bsc,cd->bsd', y, w_out[l])
    return rmsnorm(x, final_g)


_drawn_inputs = setup_inputs


def setup_inputs(seed=0):
    import zlib

    import numpy as np

    out = dict(_drawn_inputs(seed))
    spreads = {}
    factors = {'sinks': 8.0, 'gn_conv': 5.056, 'gn_attn': 4.829, 'final_g': 2.864}
    for name, (base, spread) in spreads.items():
        noise = np.random.default_rng([zlib.crc32(name.encode()), seed]).standard_normal(out[name].shape)
        drawn = base * np.exp(spread * noise) if base else spread * noise
        out[name] = __import__('jax').numpy.asarray(drawn.astype(out[name].dtype))
    for name, factor in factors.items():
        out[name] = (out[name] * factor).astype(out[name].dtype)
    return out
```

```python
from contextlib import ExitStack

import concourse.bass as bass
from concourse import mybir

F32 = mybir.dt.float32
F32R = mybir.dt.float32r
ALU = mybir.AluOpType
ACT = mybir.ActivationFunctionType
AX_X = mybir.AxisListType.X

P = 128
D_MODEL, SEQ, DEPTH = 2048, 256, 2
CHUNK, HEAD = 64, 64
CONV_WIDTH = ATTN_WIDTH = D_MODEL // 2
TILES = D_MODEL // P
HALF = TILES // 2
LANES = 2
BLOCK = LANES * P
GROUPS = CONV_WIDTH // BLOCK
GROUP_BLOCKS = 6
GROUP_UNITS = 2 * GROUP_BLOCKS
OUT_BLOCKS = D_MODEL // BLOCK
LAYER_BLOCKS = 1 + GROUPS * GROUP_BLOCKS + OUT_BLOCKS
LAYER_UNITS = 2 * LAYER_BLOCKS
UNITS = DEPTH * LAYER_UNITS
SLOTS = 4
HIGH_AHEAD, LOW_AHEAD = 3, 2
CHUNKS = SEQ // CHUNK
HEADS_AT_ONCE = 4
NEG = -1e30
EPS = 1e-5
SCALE = HEAD ** -0.5
SWAP = [*range(8, 16), *range(0, 8), *range(16, 32)]

CONV_TAPS = 3
G_TAP, G_CONV, G_ATTN, G_SINK = 0, 6, 8, 10
GROUP_COLS = 18
NORM_AT = DEPTH * GROUPS * GROUP_COLS
FINAL_AT = NORM_AT + DEPTH * TILES
PARAMS = FINAL_AT + TILES
COS_AT, SIN_AT, IDENT_AT = 0, SEQ, 2 * SEQ
CONSTS = 2 * SEQ + P


def build(nc, x_in, weights, params_in, consts_in, out):
    with ExitStack() as ctx:
        def sb(name, shape, dt=F32):
            return ctx.enter_context(nc.sbuf_tensor(name, shape, dt))

        def ps(name, shape):
            return ctx.enter_context(nc.psum_tensor(name, shape, F32))

        def sem(name):
            return ctx.enter_context(nc.semaphore(name))

        raw = [sb(f"raw{s}", [P, HALF, BLOCK]) for s in range(SLOTS)]
        w_hi = [sb(f"w_hi{s}", [P, HALF, BLOCK], F32R) for s in range(SLOTS)]
        w_lo = [sb(f"w_lo{s}", [P, HALF, BLOCK], F32R) for s in range(SLOTS)]
        x = sb("x", [P, TILES, SEQ])
        x_hi = sb("x_hi", [P, TILES, SEQ], F32R)
        x_lo = sb("x_lo", [P, TILES, SEQ], F32R)
        y_hi = sb("y_hi", [P, TILES, SEQ], F32R)
        y_lo = sb("y_lo", [P, TILES, SEQ], F32R)
        buf_a = sb("buf_a", [P, LANES, SEQ])
        buf_b = sb("buf_b", [P, LANES, SEQ])
        buf_c = sb("buf_c", [P, LANES, SEQ])
        buf_d = sb("buf_d", [P, LANES, SEQ])
        conv_in = sb("conv_in", [P, LANES, CONV_TAPS - 1 + SEQ])
        probs = [sb(f"probs{r}", [P, HEADS_AT_ONCE, P]) for r in range(2)]
        k_dup = sb("k_dup", [P, LANES, SEQ])
        v_band = sb("v_band", [P, CHUNKS, P])
        square = sb("square", [P, LANES, SEQ])
        sum_ax = sb("sum_ax", [P, LANES, SEQ])
        sum_c = sb("sum_c", [P, LANES, SEQ])
        rs_x = sb("rs_x", [P, SEQ])
        rs_ac = sb("rs_ac", [P, 2, SEQ])
        params = sb("params", [P, PARAMS])
        consts = sb("consts", [P, CONSTS])
        mean_mat = sb("mean_mat", [P, P])
        small = sb("small", [P, 64])

        acc = [ps(f"acc{p}", [P, LANES, 512]) for p in range(2)]
        scores = ps("scores", [P, 2, 512])
        turned = ps("turned", [P, 512])
        attn_ps = ps("attn_ps", [P, 512])

        cos2 = consts[:, COS_AT:COS_AT + SEQ].unsqueeze(1).to_broadcast([P, LANES, SEQ])
        sin2 = consts[:, SIN_AT:SIN_AT + SEQ].unsqueeze(1).to_broadcast([P, LANES, SEQ])
        ident = consts[:, IDENT_AT:IDENT_AT + P]
        rs_x2 = rs_x[:, :].unsqueeze(1).to_broadcast([P, LANES, SEQ])
        rs_a2 = rs_ac[:, 0, :].unsqueeze(1).to_broadcast([P, LANES, SEQ])
        rs_c2 = rs_ac[:, 1, :].unsqueeze(1).to_broadcast([P, LANES, SEQ])
        attn2 = attn_ps[:, :].rearrange("p (j n) -> p j n", j=LANES)
        v_pad = buf_c[:, :, :].rearrange("p j n -> p (j n)")
        row_max, bound, neg_max, sink_exp, row_sum, inv_den = (
            small[:, 8 * n:8 * n + 8] for n in range(6))
        eps = small[:, 63:64]

        def group_param(layer, i, at, n):
            return params[:, bass.ds(i * GROUP_COLS + (layer * GROUPS * GROUP_COLS + at), n)]

        def heads(ap):
            return ap.rearrange("p (h n) -> p h n", h=HEADS_AT_ONCE)

        raw_landed = [sem(f"raw_landed{s}") for s in range(SLOTS)]
        x_landed = [sem(f"x_landed{q}") for q in range(4)]
        params_landed, consts_landed = sem("params_landed"), sem("consts_landed")
        out_stored = sem("out_stored")
        hi_ready, lo_ready = sem("hi_ready"), sem("lo_ready")
        units_done = sem("units_done")
        acc_free = sem("acc_free")
        mean_set, eps_set, pads_set = sem("mean_set"), sem("eps_set"), sem("pads_set")
        x_high, x_split = sem("x_high"), sem("x_split")
        x_squared, x_summed = sem("x_squared"), sem("x_summed")
        x_mean, x_root, x_rs = sem("x_mean"), sem("x_root"), sem("x_rs")
        v_padded, v_scaled, v_turned, v_ready = (
            sem("v_padded"), sem("v_scaled"), sem("v_turned"), sem("v_ready"))
        k_swapped, k_cos, k_sin, k_ready = (
            sem("k_swapped"), sem("k_cos"), sem("k_sin"), sem("k_ready"))
        q_swapped, q_cos, q_sin, q_ready = (
            sem("q_swapped"), sem("q_cos"), sem("q_sin"), sem("q_ready"))
        attn_gate = sem("attn_gate")
        scores_ready, max_ready, bounded, negated, sink_less, sink_ready, exp_ready = (
            sem("scores_ready"), sem("max_ready"), sem("bounded"), sem("negated"),
            sem("sink_less"), sem("sink_ready"), sem("exp_ready"))
        den_ready, inv_ready, probs_ready = sem("den_ready"), sem("inv_ready"), sem("probs_ready")
        probs_turned, probs_back = sem("probs_turned"), sem("probs_back")
        attn_ready, attn_copied, attn_gated, attn_high, attn_split = (
            sem("attn_ready"), sem("attn_copied"), sem("attn_gated"), sem("attn_high"),
            sem("attn_split"))
        attn_squared, attn_summed = sem("attn_squared"), sem("attn_summed")
        cu_ready, tap0, tap1, tap2 = sem("cu_ready"), sem("tap0"), sem("tap1"), sem("tap2")
        conv_ready, conv_squared, conv_summed = (
            sem("conv_ready"), sem("conv_squared"), sem("conv_summed"))
        conv_gate, conv_gated, conv_high, conv_split = (
            sem("conv_gate"), sem("conv_gated"), sem("conv_high"), sem("conv_split"))
        sums_zeroed, means_ready, roots_ready, rs_ready = (
            sem("sums_zeroed"), sem("means_ready"), sem("roots_ready"), sem("rs_ready"))
        x_plus_attn, x_new, x_gained, x_final = (
            sem("x_plus_attn"), sem("x_new"), sem("x_gained"), sem("x_final"))

        def unit_of_group(layer):
            return LAYER_UNITS * layer + 2

        def unit_of_out(layer):
            return LAYER_UNITS * layer + 2 + GROUPS * GROUP_UNITS

        def block_of_group(layer):
            return LAYER_BLOCKS * layer + 1

        def block_of_out(layer):
            return LAYER_BLOCKS * layer + 1 + GROUPS * GROUP_BLOCKS

        def slot_of(at):
            return at % SLOTS

        def freed(step, at, i):
            return i * step + (at + 3)

        block = ctx.enter_context(nc.Block())

        @block.sync
        def _(sp):
            for n in range(SLOTS):
                sp.dma_start(raw[n][:, :, :], weights[n]).then_inc(raw_landed[n], 16)
            with sp.Fori(1, UNITS // SLOTS) as g:
                for s in range(SLOTS):
                    sp.wait_ge(lo_ready, g * SLOTS + (s + 1 - SLOTS))
                    sp.dma_start(raw[s][:, :, :],
                                 weights[bass.ds(g * SLOTS + s, 1)].rearrange("u p k n -> p (u k) n"),
                                 ).then_inc(raw_landed[s], 16)
            for b in range(OUT_BLOCKS):
                sp.wait_ge(x_final, b + 1)
                sp.dma_start(out[:, 2 * b:2 * b + 2, :], x[:, 2 * b:2 * b + 2, :]).then_inc(out_stored, 16)
            sp.wait_ge(out_stored, 16 * OUT_BLOCKS)

        @block.tensor
        def _(pe):
            def three_passes(where, slot, k, lane, hi, lo, tile, first, last):
                cols = slice(lane * P, lane * P + P)
                pe.matmul(where, w_hi[slot][:, k, cols], hi[:, tile, :], start=first, stop=False)
                pe.matmul(where, w_hi[slot][:, k, cols], lo[:, tile, :], start=False, stop=False)
                return pe.matmul(where, w_lo[slot][:, k, cols], hi[:, tile, :], start=False, stop=last)

            def weights_wait(step, at, i):
                pe.wait_ge(hi_ready, i * step + (at + 1))
                pe.wait_ge(lo_ready, i * step + (at + 1))

            def in_unit(step, at, i, block_step, block_at, half, middle=None):
                pair, slot = block_at % 2, slot_of(at)
                if half == 0:
                    pe.wait_ge(acc_free, i * block_step + (block_at + 1))
                weights_wait(step, at, i)
                for lane in range(LANES):
                    for k in range(HALF):
                        if middle:
                            middle(lane, k)
                        last = three_passes(acc[pair][:, lane, 0:SEQ], slot, k, lane, x_hi, x_lo,
                                            half * HALF + k, half == 0 and k == 0,
                                            half == 1 and k == HALF - 1)
                last.then_inc(units_done, 1)

            def out_unit(layer, step, at, i, block_step, block_at, half):
                pair, slot = block_at % 2, slot_of(at)
                if half == 0:
                    pe.wait_ge(acc_free, i * block_step + (block_at + 1))
                    pe.wait_ge(attn_split, GROUPS * (layer + 1))
                else:
                    pe.wait_ge(conv_split, GROUPS * (layer + 1) - 1)
                weights_wait(step, at, i)
                for lane in range(LANES):
                    for k in range(HALF):
                        if half == 1 and lane == 0 and k == HALF - LANES:
                            pe.wait_ge(conv_split, GROUPS * (layer + 1))
                        last = three_passes(acc[pair][:, lane, half * SEQ:(half + 1) * SEQ], slot, k,
                                            lane, y_hi, y_lo, half * HALF + k, k == 0, k == HALF - 1)
                last.then_inc(units_done, 1)

            def scores_of(layer):
                pe.wait_ge(k_ready, 4 * (layer + 1))
                for r in range(2):
                    rows = slice(r * HEAD, r * HEAD + HEAD)
                    for j in range(LANES):
                        for c in range(CHUNKS):
                            low = max(0, (c - 1) * CHUNK)
                            keys = k_dup[rows, j, low:(c + 1) * CHUNK]
                            at = (c // 2 * LANES + j) * P
                            last = pe.matmul(
                                scores[c % 2 * CHUNK:c % 2 * CHUNK + CHUNK, r,
                                       at + (0 if c else CHUNK):at + P],
                                buf_c[rows, j, c * CHUNK:(c + 1) * CHUNK], keys, start=True, stop=True)
                last.then_inc(scores_ready, 1)

            def turn_probs(r, it2):
                pe.wait_ge(probs_ready, it2)
                for h in range(HEADS_AT_ONCE):
                    last = pe.transpose(turned[:, h * P:(h + 1) * P], probs[r][:, h, :], ident)
                last.then_inc(probs_turned, 1)

            def values(layer, it2):
                pe.wait_ge(probs_back, it2)
                pe.wait_ge(v_ready, layer + 1)
                for c in range(CHUNKS):
                    for j in range(LANES):
                        for r in range(2):
                            last = pe.matmul(
                                attn_ps[r * HEAD:(r + 1) * HEAD, j * SEQ + c * CHUNK:j * SEQ + (c + 1) * CHUNK],
                                v_band[:, c, j * HEAD:(j + 1) * HEAD],
                                probs[r][:, c // 2 * LANES + j, c % 2 * CHUNK:c % 2 * CHUNK + CHUNK],
                                start=True, stop=True)
                last.then_inc(attn_ready, 1)

            def mean(where, sums):
                for lane in range(LANES):
                    last = pe.matmul(where, mean_mat[:, :], sums[:, lane, :], start=(lane == 0),
                                     stop=(lane == LANES - 1))
                return last

            pe.wait_ge(mean_set, 1)
            pe.wait_ge(consts_landed, 16)
            for layer in range(DEPTH):
                def x_pairs(half):
                    def wait(lane, k):
                        if lane == 0 and k % 2 == 0:
                            pe.wait_ge(x_split, OUT_BLOCKS * layer + half * HALF // 2 + k // 2 + 1)
                        if half == 1 and lane == 1 and k == 0:
                            pe.wait_ge(x_summed, OUT_BLOCKS * (layer + 1))
                            mean(turned[:, 0:SEQ], sum_ax).then_inc(x_mean, 1)
                    return wait
                for half in range(2):
                    in_unit(0, LAYER_UNITS * layer + half, 0, 0, LAYER_BLOCKS * layer, half, x_pairs(half))
                pe.wait_ge(x_root, layer + 1)
                pe.wait_ge(v_scaled, layer + 1)
                for c in range(CHUNKS):
                    last = pe.transpose(turned[:, c * P:(c + 1) * P], v_pad[:, c * CHUNK:c * CHUNK + P], ident)
                last.then_inc(v_turned, 1)

                with pe.Fori(0, GROUPS) as i:
                    it = i + (layer * GROUPS + 1)
                    it2 = i * 2 + (layer * GROUPS * 2 + 1)

                    def q_before_scores(lane, k):
                        if lane == LANES - 1 and k == HALF - 1:
                            pe.wait_ge(q_ready, it)

                    for s in range(GROUP_UNITS):
                        in_unit(GROUP_UNITS, unit_of_group(layer) + s, i,
                                GROUP_BLOCKS, block_of_group(layer) + s // 2, s % 2,
                                q_before_scores if s == 3 else None)
                        if s == 3:
                            scores_of(layer)
                        if s == 5:
                            turn_probs(0, it2)
                        if s == 6:
                            pe.wait_ge(probs_back, it2)
                            turn_probs(1, it2 + 1)
                        if s == 7:
                            values(layer, it2 + 1)

                pe.wait_ge(attn_summed, GROUPS * (layer + 1))
                pe.wait_ge(conv_summed, GROUPS * (layer + 1))
                mean(turned[:, 0:SEQ], sum_ax)
                mean(turned[:, SEQ:2 * SEQ], sum_c).then_inc(means_ready, 1)

                def out_pass(i, at=0):
                    for s in range(4):
                        out_unit(layer, 4, unit_of_out(layer) + at * 4 + s, i,
                                 2, block_of_out(layer) + at * 2 + s // 2, s % 2)
                with pe.Fori(0, OUT_BLOCKS // 2 - 1) as i:
                    out_pass(i)
                out_pass(0, OUT_BLOCKS // 2 - 1)
            pe.wait_ge(x_summed, OUT_BLOCKS * (DEPTH + 1))
            mean(turned[:, 0:SEQ], sum_ax).then_inc(x_mean, 1)

        @block.scalar
        def _(act):
            for q in range(4):
                act.dma_start(x[:, 4 * q:4 * q + 4, :], x_in[:, 4 * q:4 * q + 4, :]).then_inc(x_landed[q], 16)
                if q == 0:
                    act.dma_start(params[:, :], params_in).then_inc(params_landed, 16)
            act.dma_start(consts[:, :], consts_in).then_inc(consts_landed, 16)

            def high(step, at, i):
                slot = slot_of(at)
                if at >= SLOTS:
                    act.wait_ge(units_done, i * step + (at + 1 - SLOTS))
                act.wait_ge(raw_landed[slot], i * (16 * step // SLOTS) + 16 * (at // SLOTS + 1))
                act.activation(w_hi[slot][:, :, :], raw[slot][:, :, :], ACT.Copy).then_inc(hi_ready, 1)

            def x_high_part(layer, tile, gain_at):
                for lane in range(LANES):
                    last = act.activation(x_hi[:, bass.ds(tile + lane, 1), :], x[:, bass.ds(tile + lane, 1), :],
                                          ACT.Copy, scale=params[:, bass.ds(tile + (gain_at + lane), 1)])
                last.then_inc(x_high, 1)

            def root(layer):
                act.wait_ge(x_mean, layer + 1)
                act.activation(rs_x[:, :], turned[:, 0:SEQ], ACT.Sqrt, bias=eps,
                               scale=CONV_WIDTH / D_MODEL).then_inc(x_root, 1)

            act.wait_ge(params_landed, 16)
            for t in range(TILES // 2):
                if t % 2 == 0:
                    act.wait_ge(x_landed[t // 2], 16)
                if t in (1, 4):
                    high(0, (t - 1) // 3, 0)
                x_high_part(0, 2 * t, NORM_AT)
            high(0, 2, 0)
            bufs = [buf_a, buf_b, buf_c, buf_d]
            for t in range(TILES // 2):
                dst = bufs[t % 4] if t else sum_ax
                if t > 4:
                    act.wait_ge(x_summed, t - 3)
                act.activation(dst[:, :, :], x[:, 2 * t:2 * t + 2, :], ACT.Square).then_inc(
                    x_squared if t else x_summed, 1)
            act.wait_ge(eps_set, 1)

            for layer in range(DEPTH):
                base = LAYER_UNITS * layer
                high(0, base + HIGH_AHEAD, 0)
                high(0, base + 1 + HIGH_AHEAD, 0)
                root(layer)
                act.wait_ge(v_turned, layer + 1)
                act.activation(v_band[:, :, :].rearrange("p c n -> p (c n)"), turned[:, :],
                               ACT.Copy).then_inc(v_ready, 1)

                with act.Fori(0, GROUPS) as i:
                    it = i + (layer * GROUPS + 1)
                    it2 = i * 2 + (layer * GROUPS * 2 + 1)
                    for s in range(GROUP_UNITS):
                        if s == 4:
                            act.wait_ge(acc_free, freed(GROUP_BLOCKS, block_of_group(layer) + 1, i))
                            act.activation(buf_d[:, :, :], buf_d[:, :, :], ACT.Silu).then_inc(attn_gate, 1)
                        if s == 6 or s == 7:
                            act.wait_ge(probs_turned, it2 + (s - 6))
                            act.activation(probs[s - 6][:, :, :], heads(turned[:, :]),
                                           ACT.Copy).then_inc(probs_back, 1)
                        if s == 9:
                            act.wait_ge(attn_gated, it2 + 1)
                            act.activation(y_hi[:, bass.ds(i * 2, 2), :], buf_a[:, :, :],
                                           ACT.Copy).then_inc(attn_high, 1)
                        high(GROUP_UNITS, unit_of_group(layer) + s + HIGH_AHEAD, i)
                        if s == 4:
                            act.wait_ge(sink_less, it)
                            act.activation(sink_exp, sink_exp, ACT.Exp).then_inc(sink_ready, 1)
                            for r in range(2):
                                for h in range(HEADS_AT_ONCE):
                                    n = r * HEADS_AT_ONCE + h
                                    last = act.activation(
                                        probs[r][:, h, :], scores[:, r, h * P:(h + 1) * P], ACT.Exp,
                                        bias=neg_max[:, n:n + 1], scale=SCALE,
                                        accum_out=row_sum[:, n:n + 1])
                            last.then_inc(exp_ready, 1)
                        if s == 8:
                            act.wait_ge(attn_ready, it)
                            act.wait_ge(cu_ready, it)
                            act.activation(buf_b[:, :, :], attn2, ACT.Copy).then_inc(attn_copied, 1)
                    act.wait_ge(acc_free, freed(GROUP_BLOCKS, block_of_group(layer) + 5, i))
                    act.activation(buf_b[:, :, :], buf_b[:, :, :], ACT.Silu).then_inc(conv_gate, 1)
                    act.wait_ge(conv_gated, it2 + 1)
                    act.activation(y_hi[:, bass.ds(i * 2 + HALF, 2), :], buf_a[:, :, :],
                                   ACT.Copy).then_inc(conv_high, 1)

                act.wait_ge(means_ready, layer + 1)
                act.activation(rs_ac[:, :, :].rearrange("p g n -> p (g n)"), turned[:, :], ACT.Sqrt,
                               bias=eps).then_inc(roots_ready, 1)

                last_layer = layer == DEPTH - 1

                def x_part(i, b, at):
                    if last_layer:
                        act.wait_ge(x_squared, i * 2 + (OUT_BLOCKS * (layer + 1) + at * 2 + b))
                        for lane in range(LANES):
                            t = 4 * at + 2 * b + lane
                            last = act.activation(x[:, bass.ds(i * 4 + t, 1), :], x[:, bass.ds(i * 4 + t, 1), :],
                                                  ACT.Copy, scale=params[:, bass.ds(i * 4 + (FINAL_AT + t), 1)])
                        last.then_inc(x_gained, 1)
                    else:
                        act.wait_ge(x_new, i * 2 + (OUT_BLOCKS * layer + at * 2 + b + 1))
                        x_high_part(layer + 1, i * 4 + (4 * at + 2 * b), NORM_AT + TILES * (layer + 1))

                def out_pass(i, at=0):
                    for s in range(4):
                        n = unit_of_out(layer) + at * 4 + s + HIGH_AHEAD
                        if s == 2:
                            x_part(i, 0, at)
                        if n < UNITS:
                            high(4, n, i)
                    x_part(i, 1, at)
                with act.Fori(0, OUT_BLOCKS // 2 - 1) as i:
                    out_pass(i)
                out_pass(0, OUT_BLOCKS // 2 - 1)
            root(DEPTH)

        @block.vector
        def _(dve):
            def low(step, at, i):
                slot = slot_of(at)
                if at >= SLOTS:
                    dve.wait_ge(units_done, i * step + (at + 1 - SLOTS))
                dve.wait_ge(hi_ready, i * step + (at + 1))
                dve.tensor_tensor(w_lo[slot][:, :, :], raw[slot][:, :, :], w_hi[slot][:, :, :].bitcast(F32),
                                  ALU.subtract).then_inc(lo_ready, 1)

            def x_low_part(tile, gain_at):
                for lane in range(LANES):
                    last = dve.scalar_tensor_tensor(
                        out=x_lo[:, bass.ds(tile + lane, 1), :], in0=x[:, bass.ds(tile + lane, 1), :],
                        scalar=params[:, bass.ds(tile + (gain_at + lane), 1)],
                        in1=x_hi[:, bass.ds(tile + lane, 1), :].bitcast(F32), op0=ALU.mult, op1=ALU.subtract)
                last.then_inc(x_split, 1)

            def y_low_part(tile):
                return dve.tensor_tensor(y_lo[:, bass.ds(tile, 2), :], buf_a[:, :, :],
                                         y_hi[:, bass.ds(tile, 2), :].bitcast(F32), ALU.subtract)

            def scaled(dst, pair, rs=rs_x2, at=0):
                return dve.tensor_tensor(dst[:, :, :], acc[pair][:, :, at:at + SEQ], rs, ALU.mult)

            dve.memset(mean_mat[:, :], 1.0 / CONV_WIDTH).then_inc(mean_set, 1)
            dve.memset(eps, EPS).then_inc(eps_set, 1)
            for r in range(2):
                dve.memset(heads(scores[:, r, :])[0:CHUNK, 0:LANES, 0:CHUNK], NEG).then_inc(acc_free, 1)
            dve.memset(conv_in[:, :, 0:CONV_TAPS - 1], 0.0).then_inc(pads_set, 1)

            dve.wait_ge(params_landed, 16)
            for t in range(TILES // 2):
                dve.wait_ge(x_high, t + 1)
                x_low_part(2 * t, NORM_AT)
                if t in (1, 4):
                    low(0, (t - 1) // 3, 0)
            bufs = [buf_a, buf_b, buf_c, buf_d]
            for t in range(1, TILES // 2):
                dve.wait_ge(x_squared, t)
                dve.wait_ge(x_summed, t)
                dve.tensor_tensor(sum_ax[:, :, :], sum_ax[:, :, :], bufs[t % 4][:, :, :],
                                  ALU.add).then_inc(x_summed, 1)
            dve.wait_ge(consts_landed, 16)
            dve.wait_ge(pads_set, 1)

            def x_factor(n):
                dve.wait_ge(x_root, n)
                dve.reciprocal(rs_x[:, :], rs_x[:, :]).then_inc(x_rs, 1)

            for layer in range(DEPTH):
                base, kv_pair = LAYER_UNITS * layer, LAYER_BLOCKS * layer % 2
                low(0, base + LOW_AHEAD, 0)
                low(0, base + 1 + LOW_AHEAD, 0)
                if layer == 0:
                    dve.wait_ge(x_summed, OUT_BLOCKS)
                dve.memset(v_pad[:, 0:CHUNK], 0.0).then_inc(v_padded, 1)
                x_factor(layer + 1)
                dve.wait_ge(units_done, base + 2)
                dve.wait_ge(x_rs, layer + 1)
                dve.wait_ge(v_padded, layer + 1)
                dve.tensor_tensor(v_pad[:, CHUNK:CHUNK + SEQ], acc[kv_pair][:, 1, 0:SEQ], rs_x[:, :],
                                  ALU.mult).then_inc(v_scaled, 1)
                dve.tensor_tensor(buf_a[:, 0, :], acc[kv_pair][:, 0, 0:SEQ], rs_x[:, :],
                                  ALU.mult).then_inc(acc_free, 1)
                dve.wait_ge(acc_free, freed(0, LAYER_BLOCKS * layer, 0))
                dve.stream_shuffle(buf_b[:, 0, :], buf_a[:, 0, :], SWAP).then_inc(k_swapped, 1)
                dve.tensor_tensor(buf_a[:, 1, :], buf_a[:, 0, :], consts[:, COS_AT:COS_AT + SEQ],
                                  ALU.mult).then_inc(k_cos, 1)
                dve.wait_ge(k_swapped, layer + 1)
                dve.tensor_tensor(buf_b[:, 1, :], buf_b[:, 0, :], consts[:, SIN_AT:SIN_AT + SEQ],
                                  ALU.mult).then_inc(k_sin, 1)
                dve.wait_ge(k_cos, layer + 1)
                dve.wait_ge(k_sin, layer + 1)
                for j in range(LANES):
                    src = slice(j * HEAD, (j + 1) * HEAD)
                    for r in range(2):
                        dve.tensor_tensor(k_dup[r * HEAD:(r + 1) * HEAD, j, :], buf_a[src, 1, :],
                                          buf_b[src, 1, :], ALU.add).then_inc(k_ready, 1)
                dve.wait_ge(k_ready, 4 * (layer + 1))

                with dve.Fori(0, GROUPS) as i:
                    it = i + (layer * GROUPS + 1)
                    it2 = i * 2 + (layer * GROUPS * 2 + 1)

                    def block_done(j):
                        dve.wait_ge(units_done, i * GROUP_UNITS + (unit_of_group(layer) + 2 * j + 2))

                    def block_read(j):
                        dve.wait_ge(acc_free, freed(GROUP_BLOCKS, block_of_group(layer) + j, i))

                    def pair(j):
                        return (block_of_group(layer) + j) % 2

                    for s in range(GROUP_UNITS):
                        if s == 2:
                            block_done(0)
                            scaled(buf_a, pair(0)).then_inc(acc_free, 1)
                            block_read(0)
                            dve.tensor_tensor(buf_c[:, :, :], buf_a[:, :, :], cos2, ALU.mult).then_inc(q_cos, 1)
                            dve.stream_shuffle(buf_b[:, :, :], buf_a[:, :, :], SWAP).then_inc(q_swapped, 1)
                            dve.wait_ge(q_swapped, it)
                            dve.tensor_tensor(buf_b[:, :, :], buf_b[:, :, :], sin2, ALU.mult).then_inc(q_sin, 1)
                            dve.wait_ge(q_cos, it)
                            dve.wait_ge(q_sin, it)
                            dve.tensor_tensor(buf_c[:, :, :], buf_c[:, :, :], buf_b[:, :, :],
                                              ALU.add).then_inc(q_ready, 1)
                        if s == 4:
                            block_done(1)
                            scaled(buf_d, pair(1)).then_inc(acc_free, 1)
                        if s == 6:
                            block_done(2)
                            scaled(buf_a, pair(2)).then_inc(acc_free, 1)
                        if s == 8:
                            block_done(3)
                            scaled(buf_b, pair(3)).then_inc(acc_free, 1)
                            block_read(3)
                            dve.tensor_tensor(conv_in[:, :, CONV_TAPS - 1:], buf_a[:, :, :], buf_b[:, :, :],
                                              ALU.mult).then_inc(cu_ready, 1)
                            dve.wait_ge(cu_ready, it)
                            for tap, done in enumerate((tap0, tap1, tap2)):
                                for lane in range(LANES):
                                    src = conv_in[:, lane, tap:tap + SEQ]
                                    w = group_param(layer, i, G_TAP + tap * LANES + lane, 1)
                                    if tap == 0:
                                        dve.tensor_scalar(buf_c[:, lane, :], src, w, None,
                                                          ALU.mult).then_inc(done, 1)
                                    else:
                                        dve.wait_ge((tap0, tap1)[tap - 1], it2 + lane)
                                        dve.scalar_tensor_tensor(
                                            out=buf_c[:, lane, :], in0=src, scalar=w, in1=buf_c[:, lane, :],
                                            op0=ALU.mult, op1=ALU.add).then_inc(done, 1)
                        if s == 9:
                            dve.wait_ge(attn_copied, it)
                            for lane in range(LANES):
                                dve.scalar_tensor_tensor(
                                    out=buf_a[:, lane, :], in0=buf_b[:, lane, :],
                                    scalar=group_param(layer, i, G_ATTN + lane, 1), in1=buf_d[:, lane, :],
                                    op0=ALU.mult, op1=ALU.mult).then_inc(attn_gated, 1)
                            dve.wait_ge(attn_high, it)
                            y_low_part(i * 2).then_inc(attn_split, 1)
                        if s == 10:
                            block_done(4)
                            dve.wait_ge(attn_split, it)
                            scaled(buf_a, pair(4)).then_inc(acc_free, 1)
                            block_read(4)
                            dve.wait_ge(tap2, it2 + 1)
                            dve.tensor_tensor(buf_d[:, :, :], buf_a[:, :, :], buf_c[:, :, :],
                                              ALU.mult).then_inc(conv_ready, 1)
                        if s == 5:
                            dve.wait_ge(exp_ready, it)
                            dve.tensor_tensor(inv_den, row_sum, sink_exp, ALU.add).then_inc(den_ready, 1)
                            dve.wait_ge(den_ready, it)
                            dve.reciprocal(inv_den, inv_den).then_inc(inv_ready, 1)
                            dve.wait_ge(inv_ready, it)
                            for r in range(2):
                                by = inv_den[:, 4 * r:4 * r + 4].unsqueeze(2).to_broadcast(
                                    [P, HEADS_AT_ONCE, P])
                                dve.tensor_tensor(probs[r][:, :, :], probs[r][:, :, :], by,
                                                  ALU.mult).then_inc(probs_ready, 1)
                        low(GROUP_UNITS, unit_of_group(layer) + s + LOW_AHEAD, i)
                        if s == 4:
                            dve.wait_ge(scores_ready, it)
                            sink = group_param(layer, i, G_SINK, 8)
                            for r in range(2):
                                dve.tensor_reduce(row_max[:, 4 * r:4 * r + 4], heads(scores[:, r, :]), AX_X,
                                                  ALU.max).then_inc(max_ready, 1)
                            dve.wait_ge(max_ready, it2 + 1)
                            dve.scalar_tensor_tensor(out=bound, in0=row_max, scalar=SCALE, in1=sink,
                                                     op0=ALU.mult, op1=ALU.max).then_inc(bounded, 1)
                            dve.wait_ge(bounded, it)
                            dve.tensor_scalar(neg_max, bound, -1.0, None, ALU.mult).then_inc(negated, 1)
                            dve.tensor_tensor(sink_exp, sink, bound, ALU.subtract).then_inc(sink_less, 1)
                    block_done(5)
                    dve.wait_ge(attn_squared, it)
                    scaled(buf_b, pair(5)).then_inc(acc_free, 1)
                    dve.wait_ge(conv_gate, it)
                    dve.wait_ge(conv_squared, it)
                    for lane in range(LANES):
                        dve.scalar_tensor_tensor(
                            out=buf_a[:, lane, :], in0=buf_d[:, lane, :],
                            scalar=group_param(layer, i, G_CONV + lane, 1), in1=buf_b[:, lane, :],
                            op0=ALU.mult, op1=ALU.mult).then_inc(conv_gated, 1)
                    dve.wait_ge(conv_high, it)
                    y_low_part(i * 2 + HALF).then_inc(conv_split, 1)
                    dve.wait_ge(conv_split, it)

                dve.wait_ge(roots_ready, layer + 1)
                dve.reciprocal(rs_ac[:, :, :], rs_ac[:, :, :]).then_inc(rs_ready, 1)
                dve.wait_ge(rs_ready, layer + 1)

                last_layer = layer == DEPTH - 1

                def x_update(i, b, at):
                    pair = (block_of_out(layer) + b) % 2
                    done = i * 2 + (OUT_BLOCKS * layer + at * 2 + b + 1)
                    tiles = x[:, bass.ds(i * 4 + (4 * at + 2 * b), 2), :]
                    dve.wait_ge(units_done, i * 4 + (unit_of_out(layer) + at * 4 + 2 * b + 2))
                    scaled(buf_a, pair, rs_a2)
                    scaled(buf_b, pair, rs_c2, SEQ).then_inc(acc_free, 1)
                    dve.wait_ge(acc_free, freed(2, block_of_out(layer) + at * 2 + b, i))
                    dve.tensor_tensor(tiles, tiles, buf_a[:, :, :], ALU.add).then_inc(x_plus_attn, 1)
                    dve.wait_ge(x_plus_attn, done)
                    dve.tensor_tensor(tiles, tiles, buf_b[:, :, :], ALU.add).then_inc(x_new, 1)
                    dve.wait_ge(x_new, done)
                    if not last_layer:
                        dve.wait_ge(x_high, done + OUT_BLOCKS)
                        x_low_part(i * 4 + (4 * at + 2 * b), NORM_AT + TILES * (layer + 1))

                def out_pass(i, at=0):
                    for s in range(4):
                        n = unit_of_out(layer) + at * 4 + s + LOW_AHEAD
                        if s == 2:
                            x_update(i, 0, at)
                        if n < UNITS:
                            low(4, n, i)
                    x_update(i, 1, at)
                with dve.Fori(0, OUT_BLOCKS // 2 - 1) as i:
                    out_pass(i)
                out_pass(0, OUT_BLOCKS // 2 - 1)
            x_factor(DEPTH + 1)
            dve.wait_ge(x_rs, DEPTH + 1)
            for b in range(OUT_BLOCKS):
                dve.wait_ge(x_gained, b + 1)
                dve.tensor_tensor(x[:, 2 * b:2 * b + 2, :], x[:, 2 * b:2 * b + 2, :], rs_x2,
                                  ALU.mult).then_inc(x_final, 1)

        @block.gpsimd
        def _(pool):
            def add_square(src, sums, squared, summed, n, before):
                if before is not None:
                    pool.wait_ge(summed, before)
                pool.tensor_tensor(square[:, :, :], src, src, ALU.mult).then_inc(squared, 1)
                pool.wait_ge(squared, n)
                pool.tensor_tensor(sums[:, :, :], sums[:, :, :], square[:, :, :], ALU.add).then_inc(summed, 1)

            for layer in range(DEPTH):
                pool.wait_ge(x_mean, layer + 1)
                pool.memset(sum_ax[:, :, :], 0.0).then_inc(sums_zeroed, 1)
                pool.memset(sum_c[:, :, :], 0.0).then_inc(sums_zeroed, 1)
                pool.wait_ge(sums_zeroed, 2 * (layer + 1))
                with pool.Fori(0, GROUPS) as i:
                    it = i + (layer * GROUPS + 1)
                    pool.wait_ge(attn_copied, it)
                    add_square(buf_b[:, :, :], sum_ax, attn_squared, attn_summed, it, None)
                    pool.wait_ge(attn_summed, it)
                    pool.wait_ge(conv_ready, it)
                    add_square(buf_d[:, :, :], sum_c, conv_squared, conv_summed, it, None)
                    pool.wait_ge(conv_summed, it)
                pool.wait_ge(means_ready, layer + 1)
                pool.memset(sum_ax[:, :, :], 0.0).then_inc(mean_set, 1)
                pool.wait_ge(mean_set, layer + 2)
                with pool.Fori(0, OUT_BLOCKS) as i:
                    n = i + (OUT_BLOCKS * layer + 1)
                    pool.wait_ge(x_new, n)
                    add_square(x[:, bass.ds(i * 2, 2), :], sum_ax, x_squared, x_summed,
                               i + (OUT_BLOCKS * (layer + 1)), None)
                    pool.wait_ge(x_summed, n + OUT_BLOCKS)


def kernel(x, norm_g, w_in, conv_w, sinks, gn_conv, gn_attn, w_out, final_g):
    import numpy as np
    import concourse.bacc as bacc
    from concourse.bass_utils import run_bass_kernel_spmd

    x, norm_g, w_in, conv_w, sinks, gn_conv, gn_attn, w_out, final_g = (
        np.asarray(a) for a in (x, norm_g, w_in, conv_w, sinks, gn_conv, gn_attn, w_out, final_g))

    b_at, c_at, u_at, z_at, q_at = (n * CONV_WIDTH for n in range(5))
    k_at = q_at + ATTN_WIDTH
    za_at = k_at + 2 * P
    blocks = [(k_at, k_at + P)]
    for i in range(GROUPS):
        by_kv = [i * P, (GROUPS + i) * P]
        by_two = [2 * i * P, (2 * i + 1) * P]
        for start, lanes in ((q_at, by_kv), (za_at, by_kv), (c_at, by_two), (u_at, by_two),
                             (b_at, by_two), (z_at, by_two)):
            blocks.append(tuple(start + n for n in lanes))
    attn_rows = [CONV_WIDTH + t * P for i in range(GROUPS) for t in (i, GROUPS + i)]
    conv_rows = [t * P for t in range(HALF)]
    weights = np.empty((UNITS, P, HALF, BLOCK), w_in.dtype)
    n = 0
    for layer in range(DEPTH):
        w = w_in[layer].reshape(2, HALF, P, -1)
        for lanes in blocks:
            for half in range(2):
                for lane, at in enumerate(lanes):
                    weights[n, :, :, lane * P:(lane + 1) * P] = w[half, :, :, at:at + P].transpose(1, 0, 2)
                n += 1
        for b in range(OUT_BLOCKS):
            for rows in (attn_rows, conv_rows):
                for k, r in enumerate(rows):
                    weights[n, :, k, :] = w_out[layer, r:r + P, b * BLOCK:(b + 1) * BLOCK]
                n += 1

    def by_tile(a):
        return a.reshape(-1, P).T

    params = np.empty((P, PARAMS), x.dtype)
    for layer in range(DEPTH):
        for i in range(GROUPS):
            at = (layer * GROUPS + i) * GROUP_COLS
            for lane in range(LANES):
                two, kv = 2 * i + lane, lane * GROUPS + i
                for tap in range(CONV_TAPS):
                    params[:, at + G_TAP + tap * LANES + lane] = by_tile(conv_w[layer, tap])[:, two]
                params[:, at + G_CONV + lane] = by_tile(gn_conv[layer])[:, two]
                params[:, at + G_ATTN + lane] = by_tile(gn_attn[layer])[:, kv]
                for r in range(2):
                    for tile in range(2):
                        params[:, at + G_SINK + r * 4 + tile * LANES + lane] = sinks[
                            layer, 8 * lane + 2 * i + r]
        params[:, NORM_AT + layer * TILES:NORM_AT + (layer + 1) * TILES] = by_tile(norm_g[layer])
    params[:, FINAL_AT:FINAL_AT + TILES] = by_tile(final_g)

    half = HEAD // 8
    inv_freq = np.float32(500000.0) ** (-np.arange(half, dtype=np.float32) * np.float32(2.0)
                                        / np.float32(2 * half))
    angle = np.arange(SEQ, dtype=np.float32)[:, None] * inv_freq[None, :].astype(np.float32)
    consts = np.zeros((P, CONSTS), np.float32)
    consts[:, COS_AT:COS_AT + SEQ] = 1.0
    for p in range(P):
        d = p % HEAD
        if d < 2 * half:
            consts[p, COS_AT:COS_AT + SEQ] = np.cos(angle[:, d % half])
            consts[p, SIN_AT:SIN_AT + SEQ] = np.sin(angle[:, d % half]) * (-1.0 if d < half else 1.0)
    consts[:, IDENT_AT:IDENT_AT + P] = np.eye(P, dtype=np.float32)

    arrays = {
        "x_t": np.ascontiguousarray(x[0].T.reshape(TILES, P, SEQ).transpose(1, 0, 2)),
        "weights": weights,
        "params": params,
        "consts": consts,
    }
    nc = bacc.Bacc("TRN2", target_bir_lowering=False, num_devices=1)
    args = [nc.dram_tensor("in_" + name, a.shape, mybir.dt.from_np(a.dtype), kind="ExternalInput").ap()
            for name, a in arrays.items()]
    out = nc.dram_tensor("out_t", (P, TILES, SEQ), F32, kind="ExternalOutput").ap()
    build(nc, *args, out)
    got = run_bass_kernel_spmd(nc, [{"in_" + name: a for name, a in arrays.items()}], core_ids=[0]).results[0]["out_t"]
    return np.ascontiguousarray(got.transpose(1, 0, 2).reshape(D_MODEL, SEQ).T)[None]
```

```python
from contextlib import ExitStack

import concourse.bass as bass
from concourse import mybir

F32 = mybir.dt.float32
F32R = mybir.dt.float32r
ALU = mybir.AluOpType
ACT = mybir.ActivationFunctionType
AX_X = mybir.AxisListType.X

P = 128
D_MODEL, SEQ, DEPTH = 2048, 256, 2
CHUNK, HEAD = 64, 64
CONV_WIDTH = ATTN_WIDTH = D_MODEL // 2
TILES = D_MODEL // P
HALF = TILES // 2
LANES = 2
BLOCK = LANES * P
GROUPS = CONV_WIDTH // BLOCK
GROUP_BLOCKS = 6
GROUP_UNITS = 2 * GROUP_BLOCKS
OUT_BLOCKS = D_MODEL // BLOCK
LAYER_UNITS = 2 * (1 + GROUPS * GROUP_BLOCKS + OUT_BLOCKS)
LAYER_SUMS = 1 + GROUPS * GROUP_BLOCKS + 2 * OUT_BLOCKS
UNITS = DEPTH * LAYER_UNITS
SLOTS = 4
HIGH_AHEAD, LOW_AHEAD = 3, 2
QUARTERS = 4
CHUNKS = SEQ // CHUNK
HEADS_AT_ONCE = 4
NEG = -1e30
EPS = 1e-5
SCALE = HEAD ** -0.5
SWAP = [*range(8, 16), *range(0, 8), *range(16, 32)]

CONV_TAPS = 3
G_TAP, G_CONV, G_ATTN, G_SINK = 0, 6, 8, 10
GROUP_COLS = 18
NORM_AT = DEPTH * GROUPS * GROUP_COLS
FINAL_AT = NORM_AT + DEPTH * TILES
PARAMS = FINAL_AT + TILES
COS_AT, SIN_AT, IDENT_AT = 0, SEQ, 2 * SEQ
CONSTS = 2 * SEQ + P


def build(nc, x_in, weights, params_in, consts_in, out):
    with ExitStack() as ctx:
        def sb(name, shape, dt=F32):
            return ctx.enter_context(nc.sbuf_tensor(name, shape, dt))

        def ps(name, shape):
            return ctx.enter_context(nc.psum_tensor(name, shape, F32))

        def sem(name):
            return ctx.enter_context(nc.semaphore(name))

        raw = [sb(f"raw{s}", [P, HALF, BLOCK]) for s in range(SLOTS)]
        w_hi = [sb(f"w_hi{s}", [P, HALF, BLOCK], F32R) for s in range(SLOTS)]
        w_lo = [sb(f"w_lo{s}", [P, HALF, BLOCK], F32R) for s in range(SLOTS)]
        x = sb("x", [P, TILES, SEQ])
        x_hl = sb("x_hl", [P, TILES, 2, SEQ], F32R)
        y_hl = sb("y_hl", [P, TILES, 2, SEQ], F32R)
        buf_a = sb("buf_a", [P, LANES, SEQ])
        buf_b = sb("buf_b", [P, LANES, SEQ])
        buf_c = sb("buf_c", [P, LANES, SEQ])
        buf_d = sb("buf_d", [P, LANES, SEQ])
        conv_in = sb("conv_in", [P, LANES, CONV_TAPS - 1 + SEQ])
        probs = [sb(f"probs{r}", [P, HEADS_AT_ONCE, P]) for r in range(2)]
        k_dup = sb("k_dup", [P, LANES, SEQ])
        v_band = sb("v_band", [P, CHUNKS, P])
        square = sb("square", [P, LANES, SEQ])
        sum_ax = sb("sum_ax", [P, LANES, SEQ])
        sum_c = sb("sum_c", [P, LANES, SEQ])
        rs_x = sb("rs_x", [P, SEQ])
        rs_ac = sb("rs_ac", [P, 2, SEQ])
        params = sb("params", [P, PARAMS])
        consts = sb("consts", [P, CONSTS])
        mean_mat = sb("mean_mat", [P, P])
        small = sb("small", [P, 64])

        acc = [ps(f"acc{p}", [P, LANES, 2 * SEQ]) for p in range(2)]
        scores = ps("scores", [P, 2, 512])
        turned = ps("turned", [P, 512])
        attn_ps = ps("attn_ps", [P, 512])

        def over_lanes(row):
            return row.unsqueeze(1).to_broadcast([P, LANES, SEQ])

        cos2 = over_lanes(consts[:, COS_AT:COS_AT + SEQ])
        sin2 = over_lanes(consts[:, SIN_AT:SIN_AT + SEQ])
        ident = consts[:, IDENT_AT:IDENT_AT + P]
        rs_x2 = over_lanes(rs_x[:, :])
        rs_a2, rs_c2 = (over_lanes(rs_ac[:, g, :]) for g in range(2))
        attn2 = attn_ps[:, :].rearrange("p (j n) -> p j n", j=LANES)
        v_pad = buf_c[:, :, :].rearrange("p j n -> p (j n)")
        row_max, bound, neg_max, sink_exp, row_sum, inv_den = (
            small[:, 8 * n:8 * n + 8] for n in range(6))
        eps = small[:, 63:64]

        def group_param(layer, i, at, n):
            return params[:, bass.ds(i * GROUP_COLS + (layer * GROUPS * GROUP_COLS + at), n)]

        def heads(ap):
            return ap.rearrange("p (h n) -> p h n", h=HEADS_AT_ONCE)

        raw_landed = [sem(f"raw_landed{s}") for s in range(SLOTS)]
        quarter_landed = [sem(f"quarter_landed{q}") for q in range(2 * (QUARTERS - 1))]
        x_landed = [sem(f"x_landed{t}") for t in range(TILES // 2)]
        params_landed, consts_landed = sem("params_landed"), sem("consts_landed")
        out_stored = sem("out_stored")
        quarter_high, quarter_low = sem("quarter_high"), sem("quarter_low")
        hi_ready, lo_ready = sem("hi_ready"), sem("lo_ready")
        units_done = sem("units_done")
        low_copied = sem("low_copied")
        acc_free = sem("acc_free")
        scaled = sem("scaled")
        mean_set, eps_set, pads_set = sem("mean_set"), sem("eps_set"), sem("pads_set")
        x_high, x_low = sem("x_high"), sem("x_low")
        x_squared, x_summed = sem("x_squared"), sem("x_summed")
        early_squared, last_squared = sem("early_squared"), sem("last_squared")
        x_mean, x_root, x_rs = sem("x_mean"), sem("x_root"), sem("x_rs")
        v_padded, v_scaled, v_turned, v_ready = (
            sem("v_padded"), sem("v_scaled"), sem("v_turned"), sem("v_ready"))
        k_swapped, k_cos, k_sin, k_ready = (
            sem("k_swapped"), sem("k_cos"), sem("k_sin"), sem("k_ready"))
        q_swapped, q_cos, q_sin, q_ready = (
            sem("q_swapped"), sem("q_cos"), sem("q_sin"), sem("q_ready"))
        attn_gate = sem("attn_gate")
        scores_ready, max_ready, bounded, negated, sink_less, sink_ready, exp_ready = (
            sem("scores_ready"), sem("max_ready"), sem("bounded"), sem("negated"),
            sem("sink_less"), sem("sink_ready"), sem("exp_ready"))
        den_ready, inv_ready, probs_ready = sem("den_ready"), sem("inv_ready"), sem("probs_ready")
        probs_turned, probs_back = sem("probs_turned"), sem("probs_back")
        attn_ready, attn_copied, attn_gated, attn_high, attn_split = (
            sem("attn_ready"), sem("attn_copied"), sem("attn_gated"), sem("attn_high"),
            sem("attn_split"))
        attn_squared, attn_summed = sem("attn_squared"), sem("attn_summed")
        cu_ready, tap0, tap1, tap2 = sem("cu_ready"), sem("tap0"), sem("tap1"), sem("tap2")
        conv_ready, conv_squared, conv_summed = (
            sem("conv_ready"), sem("conv_squared"), sem("conv_summed"))
        conv_gate, conv_gated, conv_high, conv_split = (
            sem("conv_gate"), sem("conv_gated"), sem("conv_high"), sem("conv_split"))
        sums_zeroed, means_ready, roots_ready, rs_ready = (
            sem("sums_zeroed"), sem("means_ready"), sem("roots_ready"), sem("rs_ready"))
        x_plus_attn, x_new, x_gained, x_final = (
            sem("x_plus_attn"), sem("x_new"), sem("x_gained"), sem("x_final"))

        def unit_of_group(layer):
            return LAYER_UNITS * layer + 2

        def unit_of_out(layer):
            return LAYER_UNITS * layer + 2 + GROUPS * GROUP_UNITS

        def sum_of_group(layer):
            return LAYER_SUMS * layer + 1

        def sum_of_out(layer):
            return LAYER_SUMS * layer + 1 + GROUPS * GROUP_BLOCKS

        def slot_of(at):
            return at % SLOTS

        def freed(step, at, i):
            return i * step + (at + 3)

        block = ctx.enter_context(nc.Block())

        @block.sync
        def _(sp):
            for n in range(2):
                for q in range(QUARTERS):
                    landed = quarter_landed[(QUARTERS - 1) * n + q] if q < QUARTERS - 1 else raw_landed[n]
                    sp.dma_start(raw[n][:, 2 * q:2 * q + 2, :], weights[n, :, 2 * q:2 * q + 2, :],
                                 ).then_inc(landed, 16)
            for n in range(2, SLOTS):
                sp.dma_start(raw[n][:, :, :], weights[n]).then_inc(raw_landed[n], 16)
            with sp.Fori(1, UNITS // SLOTS) as g:
                for s in range(SLOTS):
                    sp.wait_ge(lo_ready, g * SLOTS + (s + 1 - SLOTS))
                    sp.dma_start(raw[s][:, :, :],
                                 weights[bass.ds(g * SLOTS + s, 1)].rearrange("u p k n -> p (u k) n"),
                                 ).then_inc(raw_landed[s], 16)
            for b in range(OUT_BLOCKS):
                sp.wait_ge(x_final, b + 1)
                sp.dma_start(out[:, 2 * b:2 * b + 2, :], x[:, 2 * b:2 * b + 2, :]).then_inc(out_stored, 16)
            sp.wait_ge(out_stored, 16 * OUT_BLOCKS)

        @block.tensor
        def _(pe):
            def unit(step, at, i, sum_step, sum_at, moving, tile, first=True, last=True, before=None):
                pair, slot = sum_at % 2, slot_of(at)
                if first:
                    pe.wait_ge(acc_free, i * sum_step + (sum_at + 1))
                if at >= 2:
                    pe.wait_ge(hi_ready, i * step + (at + 1))
                    pe.wait_ge(lo_ready, i * step + (at + 1))
                for k in range(HALF):
                    if before:
                        before(k)
                    for lane in range(LANES):
                        cols = slice(lane * P, lane * P + P)
                        pe.matmul(acc[pair][:, lane, :], w_hi[slot][:, k, cols],
                                  moving[:, tile + k, :, :], start=first and k == 0, stop=False)
                        mm = pe.matmul(acc[pair][:, lane, SEQ:], w_lo[slot][:, k, cols],
                                       moving[:, tile + k, 0, :], start=False,
                                       stop=last and k == HALF - 1)
                mm.then_inc(units_done, 1)

            def scores_of_group(layer):
                pe.wait_ge(k_ready, 4 * (layer + 1))
                for j in range(LANES):
                    for c in range(CHUNKS):
                        keys = slice(max(0, c - 1) * CHUNK, (c + 1) * CHUNK)
                        at = (c // 2 * LANES + j) * P
                        for r in range(2):
                            rows = slice(r * HEAD, r * HEAD + HEAD)
                            mm = pe.matmul(
                                scores[c % 2 * CHUNK:c % 2 * CHUNK + CHUNK, r,
                                       at + (0 if c else CHUNK):at + P],
                                buf_c[rows, j, c * CHUNK:(c + 1) * CHUNK], k_dup[rows, j, keys],
                                start=True, stop=True)
                mm.then_inc(scores_ready, 1)

            def turn_probs(r, it2):
                pe.wait_ge(probs_ready, it2)
                for h in range(HEADS_AT_ONCE):
                    mm = pe.transpose(turned[:, h * P:(h + 1) * P], probs[r][:, h, :], ident)
                mm.then_inc(probs_turned, 1)

            def values(layer, it2):
                pe.wait_ge(v_ready, layer + 1)
                pe.wait_ge(probs_back, it2)
                for c in range(CHUNKS):
                    for j in range(LANES):
                        for r in range(2):
                            mm = pe.matmul(
                                attn_ps[r * HEAD:(r + 1) * HEAD, j * SEQ + c * CHUNK:j * SEQ + (c + 1) * CHUNK],
                                v_band[:, c, j * HEAD:(j + 1) * HEAD],
                                probs[r][:, c // 2 * LANES + j, c % 2 * CHUNK:c % 2 * CHUNK + CHUNK],
                                start=True, stop=True)
                mm.then_inc(attn_ready, 1)

            def mean(where, sums, start=True, stop=True):
                for lane in range(LANES):
                    mm = pe.matmul(where, mean_mat[:, :], sums[:, lane, :], start=start and lane == 0,
                                   stop=stop and lane == LANES - 1)
                return mm

            pe.wait_ge(mean_set, 1)
            for layer in range(DEPTH):
                for half in range(2):
                    def before_kv(k):
                        if k % 2 == 0:
                            pair, q = half * HALF // 2 + k // 2, k // 2
                            pe.wait_ge(x_low, OUT_BLOCKS * layer + pair + 1)
                            if layer == 0 and q < QUARTERS - 1:
                                pe.wait_ge(quarter_low, (QUARTERS - 1) * half + q + 1)
                            elif layer == 0:
                                pe.wait_ge(lo_ready, half + 1)
                        if half == 1 and k == HALF - 1:
                            pe.wait_ge(x_summed, OUT_BLOCKS * (layer + 1))
                            mean(turned[:, 0:SEQ], sum_ax).then_inc(x_mean, 1)
                    unit(0, LAYER_UNITS * layer + half, 0, 0, LAYER_SUMS * layer, x_hl, half * HALF,
                         half == 0, half == 1, before_kv)

                def group_unit(i, s, before=None):
                    unit(GROUP_UNITS, unit_of_group(layer) + s, i, GROUP_BLOCKS,
                         sum_of_group(layer) + s // 2, x_hl, s % 2 * HALF, s % 2 == 0, s % 2 == 1, before)

                for s in range(2):
                    group_unit(0, s)
                pe.wait_ge(consts_landed, 16)
                pe.wait_ge(x_root, layer + 1)
                pe.wait_ge(v_scaled, layer + 1)
                for c in range(CHUNKS):
                    mm = pe.transpose(turned[:, c * P:(c + 1) * P], v_pad[:, c * CHUNK:c * CHUNK + P], ident)
                mm.then_inc(v_turned, 1)

                def group(i, units):
                    it = i + (layer * GROUPS + 1)
                    it2 = i * 2 + (layer * GROUPS * 2 + 1)

                    def q_before_scores(k):
                        if k == HALF - 1:
                            pe.wait_ge(q_ready, it)

                    for s in units:
                        group_unit(i, s, q_before_scores if s == 3 else None)
                        if s == 3:
                            scores_of_group(layer)
                        if s == 5:
                            turn_probs(0, it2)
                        if s == 6:
                            pe.wait_ge(probs_back, it2)
                            turn_probs(1, it2 + 1)
                        if s == 7:
                            values(layer, it2 + 1)

                with pe.Fori(0, GROUPS - 1) as i:
                    group(i, range(2, GROUP_UNITS + 2))
                group(GROUPS - 1, range(2, GROUP_UNITS))

                pe.wait_ge(attn_summed, GROUPS * (layer + 1))
                pe.wait_ge(conv_summed, GROUPS * (layer + 1))
                mean(turned[:, 0:SEQ], sum_ax)
                mean(turned[:, SEQ:2 * SEQ], sum_c).then_inc(means_ready, 1)

                def out_units(i, at):
                    def before_conv(k):
                        if k == HALF - LANES:
                            pe.wait_ge(conv_split, GROUPS * (layer + 1))
                    for s in range(4):
                        pe.wait_ge(*((conv_split, GROUPS * (layer + 1) - 1) if s % 2 else
                                     (attn_split, GROUPS * (layer + 1))))
                        unit(4, unit_of_out(layer) + at * 4 + s, i, 4, sum_of_out(layer) + at * 4 + s,
                             y_hl, s % 2 * HALF, before=before_conv if s % 2 else None)

                with pe.Fori(0, OUT_BLOCKS // 2) as i:
                    out_units(i, 0)
            pe.wait_ge(x_summed, OUT_BLOCKS * (DEPTH + 1) - 1)
            mean(turned[:, 0:SEQ], sum_ax, stop=False)
            pe.wait_ge(last_squared, 1)
            mean(turned[:, 0:SEQ], buf_c, start=False).then_inc(x_mean, 1)

        @block.scalar
        def _(act):
            act.dma_start(params[:, :], params_in).then_inc(params_landed, 16)
            for t in range(TILES // 2):
                act.dma_start(x[:, 2 * t:2 * t + 2, :], x_in[:, 2 * t:2 * t + 2, :]).then_inc(x_landed[t], 16)
            act.dma_start(consts[:, :], consts_in).then_inc(consts_landed, 16)

            def high(step, at, i):
                slot = slot_of(at)
                if at >= SLOTS:
                    act.wait_ge(units_done, i * step + (at + 1 - SLOTS))
                act.wait_ge(raw_landed[slot], i * (16 * step // SLOTS) + 16 * (at // SLOTS + 1))
                act.activation(w_hi[slot][:, :, :], raw[slot][:, :, :], ACT.Copy).then_inc(hi_ready, 1)

            def copy_low(dst, units, sum_at):
                act.wait_ge(units_done, units)
                act.activation(dst[:, :, :], acc[sum_at % 2][:, :, SEQ:], ACT.Copy).then_inc(low_copied, 1)

            def high_x(tile, gain_at):
                for lane in range(LANES):
                    a = act.activation(x_hl[:, bass.ds(tile + lane, 1), 0, :], x[:, bass.ds(tile + lane, 1), :],
                                       ACT.Copy, scale=params[:, bass.ds(tile + (gain_at + lane), 1)])
                a.then_inc(x_high, 1)

            def root(n):
                act.wait_ge(x_mean, n)
                act.activation(rs_x[:, :], turned[:, 0:SEQ], ACT.Sqrt, bias=eps,
                               scale=CONV_WIDTH / D_MODEL).then_inc(x_root, 1)

            act.wait_ge(params_landed, 16)
            for t in range(TILES // 2):
                act.wait_ge(x_landed[t], 16)
                high_x(2 * t, NORM_AT)
                n, q = t // QUARTERS, t % QUARTERS
                act.wait_ge(quarter_landed[(QUARTERS - 1) * n + q] if q < QUARTERS - 1 else raw_landed[n], 16)
                act.activation(w_hi[n][:, 2 * q:2 * q + 2, :], raw[n][:, 2 * q:2 * q + 2, :], ACT.Copy,
                               ).then_inc(quarter_high if q < QUARTERS - 1 else hi_ready, 1)
            for t, dst in zip(range(4, 8), (buf_a, buf_b, buf_c, buf_d)):
                act.activation(dst[:, :, :], x[:, 2 * t:2 * t + 2, :], ACT.Square).then_inc(early_squared, 1)
            high(0, 2, 0)
            act.wait_ge(eps_set, 1)

            for layer in range(DEPTH):
                base, first_sum = LAYER_UNITS * layer, LAYER_SUMS * layer
                high(0, base + HIGH_AHEAD, 0)
                high(0, base + 1 + HIGH_AHEAD, 0)
                if layer == 0:
                    act.wait_ge(x_summed, OUT_BLOCKS)
                copy_low(buf_a, base + 2, first_sum)
                root(layer + 1)
                for s in range(2):
                    high(0, unit_of_group(layer) + s + HIGH_AHEAD, 0)
                act.wait_ge(v_turned, layer + 1)
                act.activation(v_band[:, :, :].rearrange("p c n -> p (c n)"), turned[:, :],
                               ACT.Copy).then_inc(v_ready, 1)

                def group(i, steps):
                    it = i + (layer * GROUPS + 1)
                    it2 = i * 2 + (layer * GROUPS * 2 + 1)

                    def copy(dst, j):
                        copy_low(dst, i * GROUP_UNITS + (unit_of_group(layer) + 2 * j + 2),
                                 sum_of_group(layer) + j)

                    def wait_scaled(j):
                        act.wait_ge(scaled, i * GROUP_BLOCKS + (sum_of_group(layer) + j + 1))

                    for s in steps:
                        if s == 2:
                            act.wait_ge(lo_ready, i * GROUP_UNITS + (unit_of_group(layer) + LOW_AHEAD + 1))
                            copy(buf_a, 0)
                        if s == 4:
                            copy(buf_d, 1)
                        if s == 6:
                            act.wait_ge(q_ready, it)
                            copy(buf_a, 2)
                        if s == 8:
                            copy(buf_b, 3)
                        if s == 10:
                            act.wait_ge(attn_split, it)
                            copy(buf_a, 4)
                        if s == 12:
                            act.wait_ge(attn_squared, it)
                            copy(buf_b, 5)
                        if s == 6 or s == 7:
                            act.wait_ge(probs_turned, it2 + (s - 6))
                            act.activation(probs[s - 6][:, :, :], heads(turned[:, :]),
                                           ACT.Copy).then_inc(probs_back, 1)
                        if s == 9:
                            act.wait_ge(attn_gated, it2 + 1)
                            act.activation(y_hl[:, bass.ds(i * 2, 2), 0, :], buf_a[:, :, :],
                                           ACT.Copy).then_inc(attn_high, 1)
                        if s < 12 or len(steps) == GROUP_UNITS:
                            high(GROUP_UNITS, unit_of_group(layer) + s + HIGH_AHEAD, i)
                        if s == 4:
                            wait_scaled(1)
                            act.activation(buf_d[:, :, :], buf_d[:, :, :], ACT.Silu).then_inc(attn_gate, 1)
                            act.wait_ge(sink_less, it)
                            act.activation(sink_exp, sink_exp, ACT.Exp).then_inc(sink_ready, 1)
                            for r in range(2):
                                for h in range(HEADS_AT_ONCE):
                                    n = r * HEADS_AT_ONCE + h
                                    a = act.activation(
                                        probs[r][:, h, :], scores[:, r, h * P:(h + 1) * P], ACT.Exp,
                                        bias=neg_max[:, n:n + 1], scale=SCALE,
                                        accum_out=row_sum[:, n:n + 1])
                            a.then_inc(exp_ready, 1)
                        if s == 8:
                            act.wait_ge(attn_ready, it)
                            act.wait_ge(cu_ready, it)
                            act.activation(buf_b[:, :, :], attn2, ACT.Copy).then_inc(attn_copied, 1)
                        if s == 12:
                            wait_scaled(5)
                            act.activation(buf_b[:, :, :], buf_b[:, :, :], ACT.Silu).then_inc(conv_gate, 1)
                            act.wait_ge(conv_gated, it2 + 1)
                            act.activation(y_hl[:, bass.ds(i * 2 + HALF, 2), 0, :], buf_a[:, :, :],
                                           ACT.Copy).then_inc(conv_high, 1)

                with act.Fori(0, GROUPS - 1) as i:
                    group(i, range(2, GROUP_UNITS + 2))
                group(GROUPS - 1, range(2, GROUP_UNITS + 1))

                act.wait_ge(means_ready, layer + 1)
                act.activation(rs_ac[:, :, :].rearrange("p g n -> p (g n)"), turned[:, :], ACT.Sqrt,
                               bias=eps).then_inc(roots_ready, 1)

                last_layer = layer == DEPTH - 1

                def update_x(i, b):
                    if last_layer:
                        if isinstance(i, int) and b == 1:
                            act.wait_ge(x_new, OUT_BLOCKS * DEPTH)
                            act.activation(buf_c[:, :, :], x[:, TILES - 2:TILES, :],
                                           ACT.Square).then_inc(last_squared, 1)
                            act.wait_ge(last_squared, 1)
                        else:
                            act.wait_ge(x_squared, i * 2 + (QUARTERS + OUT_BLOCKS * layer + b + 1))
                        for lane in range(LANES):
                            t = 2 * b + lane
                            a = act.activation(x[:, bass.ds(i * 4 + t, 1), :], x[:, bass.ds(i * 4 + t, 1), :],
                                               ACT.Copy, scale=params[:, bass.ds(i * 4 + (FINAL_AT + t), 1)])
                        a.then_inc(x_gained, 1)
                    else:
                        act.wait_ge(x_new, i * 2 + (OUT_BLOCKS * layer + b + 1))
                        high_x(i * 4 + 2 * b, NORM_AT + TILES * (layer + 1))

                high(0, unit_of_out(layer) + HIGH_AHEAD, 0)
                act.wait_ge(conv_split, GROUPS * (layer + 1))

                def out_steps(i, steps):
                    for s in steps:
                        copy_low(buf_a if s % 2 else buf_b, i * 4 + (unit_of_out(layer) + s),
                                 sum_of_out(layer) + s - 1)
                        n = unit_of_out(layer) + s + HIGH_AHEAD
                        if not isinstance(i, int) or (s < 4 and n + 4 * i < UNITS):
                            high(4, n, i)
                        if s % 2 == 0:
                            update_x(i, s // 2 - 1)

                with act.Fori(0, OUT_BLOCKS // 2 - 1) as i:
                    out_steps(i, range(1, 5))
                out_steps(OUT_BLOCKS // 2 - 1, range(1, 5))
            root(DEPTH + 1)

        @block.vector
        def _(dve):
            def low(step, at, i):
                slot = slot_of(at)
                if at >= SLOTS:
                    dve.wait_ge(units_done, i * step + (at + 1 - SLOTS))
                dve.wait_ge(hi_ready, i * step + (at + 1))
                dve.tensor_tensor(w_lo[slot][:, :, :], raw[slot][:, :, :], w_hi[slot][:, :, :].bitcast(F32),
                                  ALU.subtract).then_inc(lo_ready, 1)

            def low_x(tile, gain_at):
                for lane in range(LANES):
                    v = dve.scalar_tensor_tensor(
                        out=x_hl[:, bass.ds(tile + lane, 1), 1, :], in0=x[:, bass.ds(tile + lane, 1), :],
                        scalar=params[:, bass.ds(tile + (gain_at + lane), 1)],
                        in1=x_hl[:, bass.ds(tile + lane, 1), 0, :].bitcast(F32),
                        op0=ALU.mult, op1=ALU.subtract)
                v.then_inc(x_low, 1)

            def low_y(tile):
                return dve.tensor_tensor(y_hl[:, bass.ds(tile, 2), 1, :], buf_a[:, :, :],
                                         y_hl[:, bass.ds(tile, 2), 0, :].bitcast(F32), ALU.subtract)

            def leave_psum(dst, step, at, i):
                dve.wait_ge(low_copied, i * step + (at + 1))
                dve.tensor_tensor(dst[:, :, :], acc[at % 2][:, :, 0:SEQ], dst[:, :, :],
                                  ALU.add).then_inc(acc_free, 1)

            def factor(dst, step, at, i, rs, then_wait=True):
                dve.wait_ge(acc_free, freed(step, at, i))
                dve.tensor_tensor(dst[:, :, :], dst[:, :, :], rs, ALU.mult).then_inc(scaled, 1)
                if then_wait:
                    dve.wait_ge(scaled, i * step + (at + 1))

            dve.memset(mean_mat[:, :], 1.0 / CONV_WIDTH).then_inc(mean_set, 1)
            dve.memset(eps, EPS).then_inc(eps_set, 1)
            for r in range(2):
                dve.memset(heads(scores[:, r, :])[0:CHUNK, 0:LANES, 0:CHUNK], NEG).then_inc(acc_free, 1)
            dve.memset(conv_in[:, :, 0:CONV_TAPS - 1], 0.0).then_inc(pads_set, 1)

            dve.wait_ge(params_landed, 16)
            for t in range(TILES // 2):
                dve.wait_ge(x_high, t + 1)
                low_x(2 * t, NORM_AT)
                n, q = t // QUARTERS, t % QUARTERS
                if q < QUARTERS - 1:
                    dve.wait_ge(quarter_high, (QUARTERS - 1) * n + q + 1)
                else:
                    dve.wait_ge(hi_ready, n + 1)
                part = slice(2 * q, 2 * q + 2)
                dve.tensor_tensor(w_lo[n][:, part, :], raw[n][:, part, :], w_hi[n][:, part, :].bitcast(F32),
                                  ALU.subtract).then_inc(quarter_low if q < QUARTERS - 1 else lo_ready, 1)
            dve.wait_ge(consts_landed, 16)
            dve.wait_ge(pads_set, 1)

            def factor_of_x(n):
                dve.wait_ge(x_root, n)
                dve.reciprocal(rs_x[:, :], rs_x[:, :]).then_inc(x_rs, 1)
                dve.wait_ge(x_rs, n)

            for layer in range(DEPTH):
                base, kv_sum = LAYER_UNITS * layer, LAYER_SUMS * layer
                low(0, base + LOW_AHEAD, 0)
                low(0, base + 1 + LOW_AHEAD, 0)
                if layer == 0:
                    dve.wait_ge(x_summed, OUT_BLOCKS)
                dve.memset(v_pad[:, 0:CHUNK], 0.0).then_inc(v_padded, 1)
                leave_psum(buf_a, 0, kv_sum, 0)
                factor_of_x(layer + 1)
                dve.wait_ge(v_padded, layer + 1)
                dve.wait_ge(acc_free, freed(0, kv_sum, 0))
                dve.tensor_tensor(v_pad[:, CHUNK:CHUNK + SEQ], buf_a[:, 1, :], rs_x[:, :],
                                  ALU.mult).then_inc(v_scaled, 1)
                dve.tensor_tensor(buf_a[:, 0, :], buf_a[:, 0, :], rs_x[:, :], ALU.mult).then_inc(scaled, 1)
                dve.wait_ge(scaled, kv_sum + 1)
                dve.wait_ge(v_scaled, layer + 1)
                dve.stream_shuffle(buf_b[:, 0, :], buf_a[:, 0, :], SWAP).then_inc(k_swapped, 1)
                dve.tensor_tensor(buf_a[:, 1, :], buf_a[:, 0, :], consts[:, COS_AT:COS_AT + SEQ],
                                  ALU.mult).then_inc(k_cos, 1)
                dve.wait_ge(k_swapped, layer + 1)
                dve.tensor_tensor(buf_b[:, 1, :], buf_b[:, 0, :], consts[:, SIN_AT:SIN_AT + SEQ],
                                  ALU.mult).then_inc(k_sin, 1)
                dve.wait_ge(k_cos, layer + 1)
                dve.wait_ge(k_sin, layer + 1)
                for j in range(LANES):
                    src = slice(j * HEAD, (j + 1) * HEAD)
                    for r in range(2):
                        dve.tensor_tensor(k_dup[r * HEAD:(r + 1) * HEAD, j, :], buf_a[src, 1, :],
                                          buf_b[src, 1, :], ALU.add).then_inc(k_ready, 1)
                dve.wait_ge(k_ready, 4 * (layer + 1))

                with dve.Fori(0, GROUPS) as i:
                    it = i + (layer * GROUPS + 1)
                    it2 = i * 2 + (layer * GROUPS * 2 + 1)

                    def leave(dst, j):
                        leave_psum(dst, GROUP_BLOCKS, sum_of_group(layer) + j, i)

                    def times_rs(dst, j, then_wait=True):
                        factor(dst, GROUP_BLOCKS, sum_of_group(layer) + j, i, rs_x2, then_wait)

                    for s in range(GROUP_UNITS):
                        if s == 2:
                            leave(buf_a, 0)
                            times_rs(buf_a, 0)
                            dve.wait_ge(v_turned, layer + 1)
                            dve.tensor_tensor(buf_c[:, :, :], buf_a[:, :, :], cos2, ALU.mult).then_inc(q_cos, 1)
                            dve.stream_shuffle(buf_b[:, :, :], buf_a[:, :, :], SWAP).then_inc(q_swapped, 1)
                            dve.wait_ge(q_swapped, it)
                            dve.tensor_tensor(buf_b[:, :, :], buf_b[:, :, :], sin2, ALU.mult).then_inc(q_sin, 1)
                            dve.wait_ge(q_cos, it)
                            dve.wait_ge(q_sin, it)
                            dve.tensor_tensor(buf_c[:, :, :], buf_c[:, :, :], buf_b[:, :, :],
                                              ALU.add).then_inc(q_ready, 1)
                        if s == 4:
                            leave(buf_d, 1)
                            times_rs(buf_d, 1, False)
                        if s == 6:
                            leave(buf_a, 2)
                            times_rs(buf_a, 2, False)
                        if s == 8:
                            leave(buf_b, 3)
                            times_rs(buf_b, 3)
                            dve.tensor_tensor(conv_in[:, :, CONV_TAPS - 1:], buf_a[:, :, :], buf_b[:, :, :],
                                              ALU.mult).then_inc(cu_ready, 1)
                            dve.wait_ge(cu_ready, it)
                            for tap, done in enumerate((tap0, tap1, tap2)):
                                for lane in range(LANES):
                                    src = conv_in[:, lane, tap:tap + SEQ]
                                    w = group_param(layer, i, G_TAP + tap * LANES + lane, 1)
                                    if tap == 0:
                                        dve.tensor_scalar(buf_c[:, lane, :], src, w, None,
                                                          ALU.mult).then_inc(done, 1)
                                    else:
                                        dve.wait_ge((tap0, tap1)[tap - 1], it2 + lane)
                                        dve.scalar_tensor_tensor(
                                            out=buf_c[:, lane, :], in0=src, scalar=w, in1=buf_c[:, lane, :],
                                            op0=ALU.mult, op1=ALU.add).then_inc(done, 1)
                        if s == 9:
                            dve.wait_ge(attn_copied, it)
                            for lane in range(LANES):
                                dve.scalar_tensor_tensor(
                                    out=buf_a[:, lane, :], in0=buf_b[:, lane, :],
                                    scalar=group_param(layer, i, G_ATTN + lane, 1), in1=buf_d[:, lane, :],
                                    op0=ALU.mult, op1=ALU.mult).then_inc(attn_gated, 1)
                            dve.wait_ge(attn_high, it)
                            low_y(i * 2).then_inc(attn_split, 1)
                        if s == 10:
                            leave(buf_a, 4)
                            times_rs(buf_a, 4)
                            dve.wait_ge(tap2, it2 + 1)
                            dve.tensor_tensor(buf_d[:, :, :], buf_a[:, :, :], buf_c[:, :, :],
                                              ALU.mult).then_inc(conv_ready, 1)
                        if s == 5:
                            dve.wait_ge(exp_ready, it)
                            dve.tensor_tensor(inv_den, row_sum, sink_exp, ALU.add).then_inc(den_ready, 1)
                            dve.wait_ge(den_ready, it)
                            dve.reciprocal(inv_den, inv_den).then_inc(inv_ready, 1)
                            dve.wait_ge(inv_ready, it)
                            for r in range(2):
                                by = inv_den[:, 4 * r:4 * r + 4].unsqueeze(2).to_broadcast(
                                    [P, HEADS_AT_ONCE, P])
                                dve.tensor_tensor(probs[r][:, :, :], probs[r][:, :, :], by,
                                                  ALU.mult).then_inc(probs_ready, 1)
                        low(GROUP_UNITS, unit_of_group(layer) + s + LOW_AHEAD, i)
                        if s == 4:
                            dve.wait_ge(scores_ready, it)
                            sink = group_param(layer, i, G_SINK, 8)
                            for r in range(2):
                                dve.tensor_reduce(row_max[:, 4 * r:4 * r + 4], heads(scores[:, r, :]), AX_X,
                                                  ALU.max).then_inc(max_ready, 1)
                            dve.wait_ge(max_ready, it2 + 1)
                            dve.scalar_tensor_tensor(out=bound, in0=row_max, scalar=SCALE, in1=sink,
                                                     op0=ALU.mult, op1=ALU.max).then_inc(bounded, 1)
                            dve.wait_ge(bounded, it)
                            dve.tensor_scalar(neg_max, bound, -1.0, None, ALU.mult).then_inc(negated, 1)
                            dve.tensor_tensor(sink_exp, sink, bound, ALU.subtract).then_inc(sink_less, 1)
                    leave(buf_b, 5)
                    times_rs(buf_b, 5, False)
                    dve.wait_ge(conv_squared, it)
                    dve.wait_ge(conv_gate, it)
                    for lane in range(LANES):
                        dve.scalar_tensor_tensor(
                            out=buf_a[:, lane, :], in0=buf_d[:, lane, :],
                            scalar=group_param(layer, i, G_CONV + lane, 1), in1=buf_b[:, lane, :],
                            op0=ALU.mult, op1=ALU.mult).then_inc(conv_gated, 1)
                    dve.wait_ge(conv_high, it)
                    low_y(i * 2 + HALF).then_inc(conv_split, 1)

                low(0, unit_of_out(layer) + LOW_AHEAD, 0)
                leave_psum(buf_a, 0, sum_of_out(layer), 0)
                dve.wait_ge(roots_ready, layer + 1)
                dve.reciprocal(rs_ac[:, :, :], rs_ac[:, :, :]).then_inc(rs_ready, 1)
                dve.wait_ge(rs_ready, layer + 1)
                last_layer = layer == DEPTH - 1

                def out_steps(i, steps):
                    for s in steps:
                        at = sum_of_out(layer) + s - 1
                        dst = buf_a if s % 2 else buf_b
                        if s != 1:
                            leave_psum(dst, 4, at, i)
                        factor(dst, 4, at, i, rs_a2 if s % 2 else rs_c2, s % 2 == 0)
                        b = s // 2 - 1
                        done = i * 2 + (OUT_BLOCKS * layer + b + 1)
                        if s % 2 == 0:
                            tiles = x[:, bass.ds(i * 4 + 2 * b, 2), :]
                            dve.wait_ge(x_plus_attn, done)
                            dve.tensor_tensor(tiles, tiles, buf_b[:, :, :], ALU.add).then_inc(x_new, 1)
                        n = unit_of_out(layer) + s + LOW_AHEAD
                        if not isinstance(i, int) or (s < 4 and n + 4 * i < UNITS):
                            low(4, n, i)
                        if s % 2 == 0 and not last_layer:
                            dve.wait_ge(x_new, done)
                            dve.wait_ge(x_high, done + OUT_BLOCKS)
                            low_x(i * 4 + 2 * b, NORM_AT + TILES * (layer + 1))
                        if s == 4 and not isinstance(i, int):
                            leave_psum(buf_a, 4, at + 1, i)

                with dve.Fori(0, OUT_BLOCKS // 2 - 1) as i:
                    out_steps(i, range(1, 5))
                out_steps(OUT_BLOCKS // 2 - 1, range(1, 5))
            factor_of_x(DEPTH + 1)
            for b in range(OUT_BLOCKS):
                dve.wait_ge(x_gained, b + 1)
                dve.tensor_tensor(x[:, 2 * b:2 * b + 2, :], x[:, 2 * b:2 * b + 2, :], rs_x2,
                                  ALU.mult).then_inc(x_final, 1)

        @block.gpsimd
        def _(pool):
            def add_square(src, sums, squared, squares, summed, adds):
                pool.tensor_tensor(square[:, :, :], src, src, ALU.mult).then_inc(squared, 1)
                pool.wait_ge(squared, squares)
                pool.tensor_tensor(sums[:, :, :], sums[:, :, :], square[:, :, :], ALU.add).then_inc(summed, 1)
                pool.wait_ge(summed, adds)

            zeroed = 0
            pool.memset(sum_ax[:, :, :], 0.0).then_inc(sums_zeroed, 1)
            zeroed += 1
            pool.wait_ge(sums_zeroed, zeroed)
            for t in range(QUARTERS):
                pool.wait_ge(x_landed[t], 16)
                add_square(x[:, 2 * t:2 * t + 2, :], sum_ax, x_squared, t + 1, x_summed, t + 1)
            for n, src in enumerate((buf_a, buf_b, buf_c, buf_d)):
                pool.wait_ge(early_squared, n + 1)
                pool.tensor_tensor(sum_ax[:, :, :], sum_ax[:, :, :], src[:, :, :], ALU.add).then_inc(x_summed, 1)
                pool.wait_ge(x_summed, QUARTERS + n + 1)

            for layer in range(DEPTH):
                pool.wait_ge(x_mean, layer + 1)
                pool.memset(sum_ax[:, :, :], 0.0).then_inc(sums_zeroed, 1)
                pool.memset(sum_c[:, :, :], 0.0).then_inc(sums_zeroed, 1)
                zeroed += 2
                pool.wait_ge(sums_zeroed, zeroed)
                with pool.Fori(0, GROUPS) as i:
                    it = i + (layer * GROUPS + 1)
                    pool.wait_ge(attn_copied, it)
                    add_square(buf_b[:, :, :], sum_ax, attn_squared, it, attn_summed, it)
                    pool.wait_ge(conv_ready, it)
                    add_square(buf_d[:, :, :], sum_c, conv_squared, it, conv_summed, it)
                pool.wait_ge(means_ready, layer + 1)
                pool.memset(sum_ax[:, :, :], 0.0).then_inc(sums_zeroed, 1)
                zeroed += 1
                pool.wait_ge(sums_zeroed, zeroed)

                def add_attn(i):
                    pool.wait_ge(scaled, i * 2 + (sum_of_out(layer) + 1))
                    tiles = x[:, bass.ds(i * 2, 2), :]
                    pool.tensor_tensor(tiles, tiles, buf_a[:, :, :], ALU.add).then_inc(x_plus_attn, 1)

                def out_block(i):
                    add_attn(i)
                    pool.wait_ge(x_new, i + (OUT_BLOCKS * layer + 1))
                    block_of_x = x[:, :, :].rearrange("p (b j) n -> p b (j n)", j=LANES)
                    add_square(block_of_x[:, bass.ds(i, 1), :], sum_ax,
                               x_squared, i + (QUARTERS + OUT_BLOCKS * layer + 1),
                               x_summed, i + (OUT_BLOCKS * (layer + 1) + 1))

                with pool.Fori(0, OUT_BLOCKS - 1) as i:
                    out_block(i)
                if layer < DEPTH - 1:
                    out_block(OUT_BLOCKS - 1)
                else:
                    add_attn(OUT_BLOCKS - 1)


def kernel(x, norm_g, w_in, conv_w, sinks, gn_conv, gn_attn, w_out, final_g):
    import numpy as np
    import concourse.bacc as bacc
    from concourse.bass_utils import run_bass_kernel_spmd

    x, norm_g, w_in, conv_w, sinks, gn_conv, gn_attn, w_out, final_g = (
        np.asarray(a) for a in (x, norm_g, w_in, conv_w, sinks, gn_conv, gn_attn, w_out, final_g))

    b_at, c_at, u_at, z_at, q_at = (n * CONV_WIDTH for n in range(5))
    k_at = q_at + ATTN_WIDTH
    za_at = k_at + 2 * P
    blocks = [(k_at, k_at + P)]
    for i in range(GROUPS):
        by_kv = [i * P, (GROUPS + i) * P]
        by_two = [2 * i * P, (2 * i + 1) * P]
        for start, lanes in ((q_at, by_kv), (za_at, by_kv), (c_at, by_two), (u_at, by_two),
                             (b_at, by_two), (z_at, by_two)):
            blocks.append(tuple(start + n for n in lanes))
    attn_rows = [CONV_WIDTH + t * P for i in range(GROUPS) for t in (i, GROUPS + i)]
    conv_rows = [t * P for t in range(HALF)]
    weights = np.empty((UNITS, P, HALF, BLOCK), w_in.dtype)
    n = 0
    for layer in range(DEPTH):
        w = w_in[layer].reshape(2, HALF, P, -1)
        for lanes in blocks:
            for half in range(2):
                for lane, at in enumerate(lanes):
                    weights[n, :, :, lane * P:(lane + 1) * P] = w[half, :, :, at:at + P].transpose(1, 0, 2)
                n += 1
        for b in range(OUT_BLOCKS):
            for rows in (attn_rows, conv_rows):
                for k, r in enumerate(rows):
                    weights[n, :, k, :] = w_out[layer, r:r + P, b * BLOCK:(b + 1) * BLOCK]
                n += 1

    def by_tile(a):
        return a.reshape(-1, P).T

    params = np.empty((P, PARAMS), x.dtype)
    for layer in range(DEPTH):
        for i in range(GROUPS):
            at = (layer * GROUPS + i) * GROUP_COLS
            for lane in range(LANES):
                two, kv = 2 * i + lane, lane * GROUPS + i
                for tap in range(CONV_TAPS):
                    params[:, at + G_TAP + tap * LANES + lane] = by_tile(conv_w[layer, tap])[:, two]
                params[:, at + G_CONV + lane] = by_tile(gn_conv[layer])[:, two]
                params[:, at + G_ATTN + lane] = by_tile(gn_attn[layer])[:, kv]
                for r in range(2):
                    for tile in range(2):
                        params[:, at + G_SINK + r * 4 + tile * LANES + lane] = sinks[
                            layer, 8 * lane + 2 * i + r]
        params[:, NORM_AT + layer * TILES:NORM_AT + (layer + 1) * TILES] = by_tile(norm_g[layer])
    params[:, FINAL_AT:FINAL_AT + TILES] = by_tile(final_g)

    half = HEAD // 8
    inv_freq = np.float32(500000.0) ** (-np.arange(half, dtype=np.float32) * np.float32(2.0)
                                        / np.float32(2 * half))
    angle = np.arange(SEQ, dtype=np.float32)[:, None] * inv_freq[None, :].astype(np.float32)
    consts = np.zeros((P, CONSTS), np.float32)
    consts[:, COS_AT:COS_AT + SEQ] = 1.0
    for p in range(P):
        d = p % HEAD
        if d < 2 * half:
            consts[p, COS_AT:COS_AT + SEQ] = np.cos(angle[:, d % half])
            consts[p, SIN_AT:SIN_AT + SEQ] = np.sin(angle[:, d % half]) * (-1.0 if d < half else 1.0)
    consts[:, IDENT_AT:IDENT_AT + P] = np.eye(P, dtype=np.float32)

    arrays = {
        "x_t": np.ascontiguousarray(x[0].T.reshape(TILES, P, SEQ).transpose(1, 0, 2)),
        "weights": weights,
        "params": params,
        "consts": consts,
    }
    nc = bacc.Bacc("TRN2", target_bir_lowering=False, num_devices=1)
    args = [nc.dram_tensor("in_" + name, a.shape, mybir.dt.from_np(a.dtype), kind="ExternalInput").ap()
            for name, a in arrays.items()]
    out = nc.dram_tensor("out_t", (P, TILES, SEQ), F32, kind="ExternalOutput").ap()
    build(nc, *args, out)
    got = run_bass_kernel_spmd(nc, [{"in_" + name: a for name, a in arrays.items()}], core_ids=[0]).results[0]["out_t"]
    return np.ascontiguousarray(got.transpose(1, 0, 2).reshape(D_MODEL, SEQ).T)[None]
```

```python
from contextlib import ExitStack

import concourse.bass as bass
from concourse import mybir

F32 = mybir.dt.float32
F32R = mybir.dt.float32r
ALU = mybir.AluOpType
ACT = mybir.ActivationFunctionType
AX_X = mybir.AxisListType.X

P = 128
D_MODEL, SEQ, DEPTH = 2048, 256, 2
CHUNK, HEAD = 64, 64
CONV_WIDTH = ATTN_WIDTH = D_MODEL // 2
TILES = D_MODEL // P
HALF = TILES // 2
LANES = 2
BLOCK = LANES * P
GROUPS = CONV_WIDTH // BLOCK
GROUP_BLOCKS = 6
GROUP_UNITS = 2 * GROUP_BLOCKS
OUT_BLOCKS = D_MODEL // BLOCK
LAYER_UNITS = 2 * (1 + GROUPS * GROUP_BLOCKS + OUT_BLOCKS)
LAYER_SUMS = 1 + GROUPS * GROUP_BLOCKS + 2 * OUT_BLOCKS
UNITS = DEPTH * LAYER_UNITS
SLOTS = 4
HIGH_AHEAD, LOW_AHEAD = 3, 2
PARTS = (4, 4, 2, 2)
WARM_UP = 14
EARLY_SQUARES = (6, 7)
CHUNKS = SEQ // CHUNK
NEG = -1e30
EPS = 1e-5
SCALE = HEAD ** -0.5
SWAP = [*range(8, 16), *range(0, 8), *range(16, 32)]

CONV_TAPS = 3
G_TAP, G_CONV, G_ATTN, G_SINK = 0, 6, 8, 10
GROUP_COLS = 18
NORM_AT = DEPTH * GROUPS * GROUP_COLS
FINAL_AT = NORM_AT + DEPTH * TILES
PARAMS = FINAL_AT + TILES
COS_AT, SIN_AT, IDENT_AT = 0, SEQ, 2 * SEQ
CONSTS = 2 * SEQ + P


def build(nc, x_in, weights, params_in, consts_in, out):
    with ExitStack() as ctx:
        def sb(name, shape, dt=F32):
            return ctx.enter_context(nc.sbuf_tensor(name, shape, dt))

        def ps(name, shape):
            return ctx.enter_context(nc.psum_tensor(name, shape, F32))

        def sem(name):
            return ctx.enter_context(nc.semaphore(name))

        raw = [sb(f"raw{s}", [P, HALF, BLOCK]) for s in range(SLOTS)]
        w_hi = [sb(f"w_hi{s}", [P, HALF, BLOCK], F32R) for s in range(SLOTS)]
        w_lo = [sb(f"w_lo{s}", [P, HALF, BLOCK], F32R) for s in range(SLOTS)]
        x = sb("x", [P, TILES, SEQ])
        x_hl = sb("x_hl", [P, TILES, 2, SEQ], F32R)
        y_hl = sb("y_hl", [P, TILES, 2, SEQ], F32R)
        buf_a = sb("buf_a", [P, LANES, SEQ])
        buf_b = sb("buf_b", [P, LANES, SEQ])
        buf_c = sb("buf_c", [P, LANES, SEQ])
        buf_d = sb("buf_d", [P, LANES, SEQ])
        conv_in = sb("conv_in", [P, LANES, CONV_TAPS - 1 + SEQ])
        probs = [sb(f"probs{r}", [P, CHUNKS, P]) for r in range(2)]
        k_dup = sb("k_dup", [P, LANES, SEQ])
        v_band = sb("v_band", [P, CHUNKS, P])
        square = sb("square", [P, LANES, SEQ])
        sum_ax = sb("sum_ax", [P, LANES, SEQ])
        sum_c = sb("sum_c", [P, LANES, SEQ])
        rs_x = sb("rs_x", [P, SEQ])
        rs_ac = sb("rs_ac", [P, 2, SEQ])
        params = sb("params", [P, PARAMS])
        consts = sb("consts", [P, CONSTS])
        mean_mat = sb("mean_mat", [P, P])
        small = sb("small", [P, 64])

        acc = [ps(f"acc{p}", [P, LANES, 2 * SEQ]) for p in range(2)]
        scores = ps("scores", [P, 2, 512])
        turned = ps("turned", [P, 512])
        attn_ps = ps("attn_ps", [P, 512])

        def over_lanes(row):
            return row.unsqueeze(1).to_broadcast([P, LANES, SEQ])

        cos2 = over_lanes(consts[:, COS_AT:COS_AT + SEQ])
        sin2 = over_lanes(consts[:, SIN_AT:SIN_AT + SEQ])
        ident = consts[:, IDENT_AT:IDENT_AT + P]
        rs_x2 = over_lanes(rs_x[:, :])
        rs_a2, rs_c2 = (over_lanes(rs_ac[:, g, :]) for g in range(2))
        attn2 = attn_ps[:, :].rearrange("p (j n) -> p j n", j=LANES)
        v_pad = buf_c[:, :, :].rearrange("p j n -> p (j n)")
        row_max, bound, neg_max, sink_exp, row_sum, inv_den = (
            small[:, 8 * n:8 * n + 8] for n in range(6))
        eps = small[:, 63:64]

        def group_param(layer, i, at, n):
            return params[:, bass.ds(i * GROUP_COLS + (layer * GROUPS * GROUP_COLS + at), n)]

        q_rows = buf_a[:, :, :].rearrange("p j n -> p (j n)")
        q_by_lane = q_rows.rearrange("p (c j n) -> p j c n", c=CHUNKS, j=LANES)

        def by_lane(buf):
            return buf[:, :, :].rearrange("p j (c n) -> p j c n", c=CHUNKS)

        def chunks(ap):
            return ap.rearrange("p (c n) -> p c n", c=CHUNKS)

        raw_landed = [sem(f"raw_landed{s}") for s in range(SLOTS)]
        part_landed = [[sem(f"part_landed{n}_{q}") for q in range(PARTS[n] - 1)] + [raw_landed[n]]
                       for n in range(SLOTS)]
        x_landed = [sem(f"x_landed{t}") for t in range(TILES // 2)]
        params_landed, consts_landed = sem("params_landed"), sem("consts_landed")
        out_stored = sem("out_stored")
        part_high, part_low = sem("part_high"), sem("part_low")
        hi_ready, lo_ready = sem("hi_ready"), sem("lo_ready")
        units_done = sem("units_done")
        lane_done = sem("lane_done")
        low_copied = sem("low_copied")
        acc_free = sem("acc_free")
        scaled = sem("scaled")
        mean_set, eps_set, pads_set = sem("mean_set"), sem("eps_set"), sem("pads_set")
        x_high, x_low = sem("x_high"), sem("x_low")
        x_squared, x_summed = sem("x_squared"), sem("x_summed")
        x_folded, groups_folded = sem("x_folded"), sem("groups_folded")
        early_squared, last_squared = sem("early_squared"), sem("last_squared")
        x_mean, x_root, x_rs = sem("x_mean"), sem("x_root"), sem("x_rs")
        v_padded, v_scaled, v_turned, v_ready = (
            sem("v_padded"), sem("v_scaled"), sem("v_turned"), sem("v_ready"))
        k_swapped, k_cos, k_sin, k_ready = (
            sem("k_swapped"), sem("k_cos"), sem("k_sin"), sem("k_ready"))
        q_swapped, q_cos, q_sin, q_ready = (
            sem("q_swapped"), sem("q_cos"), sem("q_sin"), sem("q_ready"))
        attn_gate = sem("attn_gate")
        scores_ready, max_ready, bounded, negated, sink_less, sink_ready, exp_ready = (
            sem("scores_ready"), sem("max_ready"), sem("bounded"), sem("negated"),
            sem("sink_less"), sem("sink_ready"), sem("exp_ready"))
        den_ready, inv_ready, probs_ready = sem("den_ready"), sem("inv_ready"), sem("probs_ready")
        probs_turned, probs_back = sem("probs_turned"), sem("probs_back")
        attn_ready, attn_copied, attn_gated, attn_high, attn_split = (
            sem("attn_ready"), sem("attn_copied"), sem("attn_gated"), sem("attn_high"),
            sem("attn_split"))
        attn_squared, attn_summed = sem("attn_squared"), sem("attn_summed")
        cu_ready, tap0, tap1, tap2 = sem("cu_ready"), sem("tap0"), sem("tap1"), sem("tap2")
        conv_ready, conv_squared, conv_summed = (
            sem("conv_ready"), sem("conv_squared"), sem("conv_summed"))
        conv_gate, conv_gated, conv_high, conv_split = (
            sem("conv_gate"), sem("conv_gated"), sem("conv_high"), sem("conv_split"))
        sums_zeroed, means_ready, roots_ready, rs_ready = (
            sem("sums_zeroed"), sem("means_ready"), sem("roots_ready"), sem("rs_ready"))
        x_plus_attn, x_new, x_gained, x_final = (
            sem("x_plus_attn"), sem("x_new"), sem("x_gained"), sem("x_final"))

        def unit_of_group(layer):
            return LAYER_UNITS * layer + 2

        def unit_of_out(layer):
            return LAYER_UNITS * layer + 2 + GROUPS * GROUP_UNITS

        def sum_of_group(layer):
            return LAYER_SUMS * layer + 1

        def sum_of_out(layer):
            return LAYER_SUMS * layer + 1 + GROUPS * GROUP_BLOCKS

        def slot_of(at):
            return at % SLOTS

        def freed(step, at, i):
            return i * step + (at + 3)

        def part_rows(n, q):
            rows = HALF // PARTS[n]
            return slice(q * rows, (q + 1) * rows)

        def part_done(n, q, part_sem, unit_sem):
            if q == PARTS[n] - 1:
                return unit_sem, n + 1
            return part_sem, sum(parts - 1 for parts in PARTS[:n]) + q + 1

        def load_x(engine, t):
            tiles = slice(2 * t, 2 * t + 2)
            engine.dma_start(x[:, tiles, :], x_in[:, tiles, :]).then_inc(x_landed[t], 16)

        block = ctx.enter_context(nc.Block())

        @block.sync
        def _(sp):
            def load_part(n, q):
                rows = part_rows(n, q)
                sp.dma_start(raw[n][:, rows, :], weights[n, :, rows, :]).then_inc(part_landed[n][q], 16)

            load_part(0, 0)
            for t in range(1, TILES // 2):
                load_part(t // PARTS[0], t % PARTS[0])
                load_x(sp, t)
            for n in range(2, SLOTS):
                for q in range(PARTS[n]):
                    load_part(n, q)
            sp.dma_start(consts[:, :], consts_in).then_inc(consts_landed, 16)
            with sp.Fori(1, UNITS // SLOTS) as g:
                for s in range(SLOTS):
                    sp.wait_ge(lo_ready, g * SLOTS + (s + 1 - SLOTS))
                    sp.dma_start(raw[s][:, :, :],
                                 weights[bass.ds(g * SLOTS + s, 1)].rearrange("u p k n -> p (u k) n"),
                                 ).then_inc(raw_landed[s], 16)
            for b in range(OUT_BLOCKS):
                sp.wait_ge(x_final, b + 1)
                sp.dma_start(out[:, 2 * b:2 * b + 2, :], x[:, 2 * b:2 * b + 2, :]).then_inc(out_stored, 16)
            sp.wait_ge(out_stored, 16 * OUT_BLOCKS)

        @block.tensor
        def _(pe):
            def unit(step, at, i, sum_step, sum_at, moving, tile, first=True, last=True, before=None,
                     lane_by_lane=False):
                pair, slot = sum_at % 2, slot_of(at)
                if first:
                    pe.wait_ge(acc_free, i * sum_step + (sum_at + 1))
                if at >= SLOTS:
                    pe.wait_ge(hi_ready, i * step + (at + 1))
                    pe.wait_ge(lo_ready, i * step + (at + 1))
                order = [(k, lane) for k in range(HALF) for lane in range(LANES)]
                if lane_by_lane:
                    order.sort(key=lambda k_lane: k_lane[1])
                for k, lane in order:
                    if before and lane == 0:
                        before(k)
                    cols = slice(lane * P, lane * P + P)
                    pe.matmul(acc[pair][:, lane, :], w_hi[slot][:, k, cols],
                              moving[:, tile + k, :, :], start=first and k == 0, stop=False)
                    mm = pe.matmul(acc[pair][:, lane, SEQ:], w_lo[slot][:, k, cols],
                                   moving[:, tile + k, 0, :], start=False,
                                   stop=last and k == HALF - 1)
                    if lane_by_lane and k == HALF - 1:
                        mm.then_inc(lane_done, 1)
                if not lane_by_lane:
                    mm.then_inc(units_done, 1)

            def scores_of_group(layer, kv):
                pe.wait_ge(k_ready, 4 * (layer + 1))
                for c in range(CHUNKS):
                    keys = slice(max(0, c - 1) * CHUNK, (c + 1) * CHUNK)
                    for r in range(2):
                        rows = slice(r * HEAD, r * HEAD + HEAD)
                        mm = pe.matmul(scores[:, r, c * P + (0 if c else CHUNK):(c + 1) * P],
                                       q_rows[rows, c * P:(c + 1) * P], k_dup[rows, kv, keys],
                                       start=True, stop=True)
                mm.then_inc(scores_ready, 1)

            def turn_probs(r, it2):
                pe.wait_ge(probs_ready, it2)
                for c in range(CHUNKS):
                    mm = pe.transpose(turned[:, c * P:(c + 1) * P], probs[r][:, c, :], ident)
                mm.then_inc(probs_turned, 1)

            def values(layer, kv, it2):
                pe.wait_ge(v_ready, layer + 1)
                pe.wait_ge(probs_back, it2)
                for c in range(CHUNKS):
                    for r in range(2):
                        mm = pe.matmul(attn2[r * HEAD:(r + 1) * HEAD, :, c * CHUNK:(c + 1) * CHUNK],
                                       v_band[:, c, kv * HEAD:(kv + 1) * HEAD], probs[r][:, c, :],
                                       start=True, stop=True)
                mm.then_inc(attn_ready, 1)

            def mean(where, squares, start=True, stop=True):
                return pe.matmul(where, mean_mat[:, :], squares, start=start, stop=stop)

            pe.wait_ge(mean_set, 1)
            for _ in range(WARM_UP):
                pe.matmul(turned[:, 0:P], mean_mat[:, :], mean_mat[:, :], start=True, stop=True)
            for layer in range(DEPTH):
                def wait_part(n, k):
                    if layer == 0 and k % (HALF // PARTS[n]) == 0:
                        pe.wait_ge(*part_done(n, k // (HALF // PARTS[n]), part_low, lo_ready))

                for half in range(2):
                    def before_kv(k):
                        if k % 2 == 0:
                            pe.wait_ge(x_low, OUT_BLOCKS * layer + (half * HALF + k) // 2 + 1)
                        wait_part(half, k)
                    unit(0, LAYER_UNITS * layer + half, 0, 0, LAYER_SUMS * layer, x_hl, half * HALF,
                         half == 0, half == 1, before_kv)

                def group_unit(i, s, before=None):
                    unit(GROUP_UNITS, unit_of_group(layer) + s, i, GROUP_BLOCKS,
                         sum_of_group(layer) + s // 2, x_hl, s % 2 * HALF, s % 2 == 0, s % 2 == 1, before)

                for s in range(2):
                    def before_q(k):
                        wait_part(2 + s, k)
                        if (s, k) == ((1, 1) if layer == 0 else (0, 0)):
                            pe.wait_ge(x_folded, layer + 1)
                            mean(turned[:, 0:SEQ], sum_ax[:, 0, :]).then_inc(x_mean, 1)
                    group_unit(0, s, before_q)
                pe.wait_ge(consts_landed, 16)
                pe.wait_ge(x_root, layer + 1)
                pe.wait_ge(v_scaled, layer + 1)
                for c in range(CHUNKS):
                    mm = pe.transpose(turned[:, c * P:(c + 1) * P], v_pad[:, c * CHUNK:c * CHUNK + P], ident)
                mm.then_inc(v_turned, 1)

                def group(i, kv, units):
                    it = i + (layer * GROUPS + 1)
                    it2 = i * 2 + (layer * GROUPS * 2 + 1)

                    def first_turn_inside(k):
                        if k == 2:
                            turn_probs(0, it2)

                    for s in units:
                        group_unit(i, s, first_turn_inside if s == 6 else None)
                        if s == 3:
                            pe.wait_ge(q_ready, it)
                            scores_of_group(layer, kv)
                        if s == 6:
                            pe.wait_ge(probs_back, it2)
                            turn_probs(1, it2 + 1)
                        if s == 7:
                            values(layer, kv, it2 + 1)

                with pe.Fori(0, GROUPS // 2) as i:
                    group(i, 0, range(2, GROUP_UNITS + 2))
                group(GROUPS // 2, 1, range(2, GROUP_UNITS + 2))
                group(GROUPS - 1, 1, range(2, GROUP_UNITS))

                pe.wait_ge(groups_folded, 2 * (layer + 1))
                mean(turned[:, 0:SEQ], sum_ax[:, 0, :])
                mean(turned[:, SEQ:2 * SEQ], sum_c[:, 0, :]).then_inc(means_ready, 1)

                def out_units(i):
                    def before_conv(k):
                        if k == HALF - LANES:
                            pe.wait_ge(conv_split, GROUPS * (layer + 1))
                    for s in range(4):
                        pe.wait_ge(*((conv_split, GROUPS * (layer + 1) - 1) if s % 2 else
                                     (attn_split, GROUPS * (layer + 1))))
                        last_unit = layer == DEPTH - 1 and isinstance(i, int) and s == 3
                        unit(4, unit_of_out(layer) + s, i, 4, sum_of_out(layer) + s, y_hl, s % 2 * HALF,
                             before=before_conv if s % 2 and not last_unit else None,
                             lane_by_lane=last_unit)

                with pe.Fori(0, OUT_BLOCKS // 2 - 1) as i:
                    out_units(i)
                out_units(OUT_BLOCKS // 2 - 1)
            pe.wait_ge(x_folded, DEPTH + 1)
            mean(turned[:, 0:SEQ], sum_ax[:, 0, :], stop=False)
            for lane in range(LANES):
                pe.wait_ge(last_squared, lane + 1)
                mm = mean(turned[:, 0:SEQ], buf_c[:, lane, :], start=False, stop=lane == LANES - 1)
            mm.then_inc(x_mean, 1)

        @block.scalar
        def _(act):
            act.dma_start(params[:, :], params_in).then_inc(params_landed, 16)
            load_x(act, 0)

            def high(step, at, i):
                slot = slot_of(at)
                if at >= SLOTS:
                    act.wait_ge(units_done, i * step + (at + 1 - SLOTS))
                act.wait_ge(raw_landed[slot], i * (16 * step // SLOTS) + 16 * (at // SLOTS + 1))
                act.activation(w_hi[slot][:, :, :], raw[slot][:, :, :], ACT.Copy).then_inc(hi_ready, 1)

            def copy_low(dst, units, sum_at):
                act.wait_ge(units_done, units)
                act.activation(dst[:, :, :], acc[sum_at % 2][:, :, SEQ:], ACT.Copy).then_inc(low_copied, 1)

            def high_x(tile, gain_at):
                for lane in range(LANES):
                    a = act.activation(x_hl[:, bass.ds(tile + lane, 1), 0, :], x[:, bass.ds(tile + lane, 1), :],
                                       ACT.Copy, scale=params[:, bass.ds(tile + (gain_at + lane), 1)])
                a.then_inc(x_high, 1)

            def root(n):
                act.wait_ge(x_mean, n)
                act.activation(rs_x[:, :], turned[:, 0:SEQ], ACT.Sqrt, bias=eps,
                               scale=CONV_WIDTH / D_MODEL).then_inc(x_root, 1)

            def high_part(n, q):
                rows = part_rows(n, q)
                act.wait_ge(part_landed[n][q], 16)
                act.activation(w_hi[n][:, rows, :], raw[n][:, rows, :], ACT.Copy,
                               ).then_inc(part_done(n, q, part_high, hi_ready)[0], 1)

            for t in range(TILES // 2):
                high_part(t // PARTS[0], t % PARTS[0])
                if t == 0:
                    act.wait_ge(params_landed, 16)
                act.wait_ge(x_landed[t], 16)
                high_x(2 * t, NORM_AT)
            for q in range(PARTS[2]):
                high_part(2, q)
            for t, dst in zip(EARLY_SQUARES, (buf_b, buf_d)):
                act.activation(dst[:, :, :], x[:, 2 * t:2 * t + 2, :], ACT.Square).then_inc(early_squared, 1)
            for q in range(PARTS[3]):
                high_part(3, q)
            act.wait_ge(eps_set, 1)

            for layer in range(DEPTH):
                base, first_sum = LAYER_UNITS * layer, LAYER_SUMS * layer
                if layer:
                    high(0, base + HIGH_AHEAD, 0)
                copy_low(buf_a, base + 2, first_sum)
                root(layer + 1)
                for s in range(-1, 2):
                    high(0, unit_of_group(layer) + s + HIGH_AHEAD, 0)
                act.wait_ge(v_turned, layer + 1)
                act.activation(v_band[:, :, :].rearrange("p c n -> p (c n)"), turned[:, :],
                               ACT.Copy).then_inc(v_ready, 1)

                def group(i, steps):
                    it = i + (layer * GROUPS + 1)
                    it2 = i * 2 + (layer * GROUPS * 2 + 1)

                    def copy(dst, j):
                        copy_low(dst, i * GROUP_UNITS + (unit_of_group(layer) + 2 * j + 2),
                                 sum_of_group(layer) + j)

                    def wait_scaled(j):
                        act.wait_ge(scaled, i * GROUP_BLOCKS + (sum_of_group(layer) + j + 1))

                    for s in steps:
                        if s == 2:
                            act.wait_ge(scaled, i * GROUP_BLOCKS + sum_of_group(layer))
                            copy(buf_c, 0)
                        if s == 4:
                            copy(buf_d, 1)
                        if s == 6:
                            act.wait_ge(scores_ready, it)
                            copy(buf_a, 2)
                        if s == 8:
                            copy(buf_b, 3)
                        if s == 10:
                            act.wait_ge(attn_split, it)
                            copy(buf_a, 4)
                        if s == 12:
                            act.wait_ge(attn_squared, it)
                            copy(buf_b, 5)
                        if s == 6 or s == 7:
                            act.wait_ge(probs_turned, it2 + (s - 6))
                            act.activation(probs[s - 6][:, :, :], chunks(turned[:, :]),
                                           ACT.Copy).then_inc(probs_back, 1)
                        if s == 9:
                            act.wait_ge(attn_gated, it2 + 1)
                            act.activation(y_hl[:, bass.ds(i * 2, 2), 0, :], buf_a[:, :, :],
                                           ACT.Copy).then_inc(attn_high, 1)
                        if s < 12 or len(steps) == GROUP_UNITS:
                            high(GROUP_UNITS, unit_of_group(layer) + s + HIGH_AHEAD, i)
                        if s == 4:
                            wait_scaled(1)
                            act.activation(buf_d[:, :, :], buf_d[:, :, :], ACT.Silu).then_inc(attn_gate, 1)
                            act.wait_ge(sink_less, it)
                            act.activation(sink_exp, sink_exp, ACT.Exp).then_inc(sink_ready, 1)
                            for r in range(2):
                                for c in range(CHUNKS):
                                    n = r * CHUNKS + c
                                    a = act.activation(
                                        probs[r][:, c, :], scores[:, r, c * P:(c + 1) * P], ACT.Exp,
                                        bias=neg_max[:, n:n + 1], scale=SCALE,
                                        accum_out=row_sum[:, n:n + 1])
                            a.then_inc(exp_ready, 1)
                        if s == 8:
                            act.wait_ge(attn_ready, it)
                            act.wait_ge(cu_ready, it)
                            act.activation(buf_b[:, :, :], attn2, ACT.Copy).then_inc(attn_copied, 1)
                        if s == 12:
                            wait_scaled(5)
                            act.activation(buf_b[:, :, :], buf_b[:, :, :], ACT.Silu).then_inc(conv_gate, 1)
                            act.wait_ge(conv_gated, it2 + 1)
                            act.activation(y_hl[:, bass.ds(i * 2 + HALF, 2), 0, :], buf_a[:, :, :],
                                           ACT.Copy).then_inc(conv_high, 1)

                with act.Fori(0, GROUPS - 1) as i:
                    group(i, range(2, GROUP_UNITS + 2))
                group(GROUPS - 1, range(2, GROUP_UNITS + 1))

                act.wait_ge(means_ready, layer + 1)
                act.activation(rs_ac[:, :, :].rearrange("p g n -> p (g n)"), turned[:, :], ACT.Sqrt,
                               bias=eps).then_inc(roots_ready, 1)

                last_layer = layer == DEPTH - 1

                def update_x(i, b):
                    if last_layer:
                        act.wait_ge(x_squared, i * 2 + (EARLY_SQUARES[0] + OUT_BLOCKS * layer + b + 1))
                        for lane in range(LANES):
                            t = 2 * b + lane
                            a = act.activation(x[:, bass.ds(i * 4 + t, 1), :], x[:, bass.ds(i * 4 + t, 1), :],
                                               ACT.Copy, scale=params[:, bass.ds(i * 4 + (FINAL_AT + t), 1)])
                        a.then_inc(x_gained, 1)
                    else:
                        act.wait_ge(x_new, i * 2 + (OUT_BLOCKS * layer + b + 1))
                        high_x(i * 4 + 2 * b, NORM_AT + TILES * (layer + 1))

                high(0, unit_of_out(layer) + HIGH_AHEAD, 0)
                act.wait_ge(conv_split, GROUPS * (layer + 1))

                def last_step():
                    for lane in range(LANES):
                        act.wait_ge(lane_done, lane + 1)
                        act.activation(buf_b[:, lane, :], acc[(DEPTH * LAYER_SUMS - 1) % 2][:, lane, SEQ:],
                                       ACT.Copy).then_inc(low_copied, 1)
                    for lane in range(LANES):
                        tile = x[:, TILES - LANES + lane, :]
                        act.wait_ge(x_new, OUT_BLOCKS * DEPTH + lane)
                        act.activation(buf_c[:, lane, :], tile, ACT.Square).then_inc(last_squared, 1)
                    for lane in range(LANES):
                        tile, gain = x[:, TILES - LANES + lane, :], FINAL_AT + TILES - LANES + lane
                        act.wait_ge(last_squared, LANES)
                        a = act.activation(tile, tile, ACT.Copy, scale=params[:, gain:gain + 1])
                    a.then_inc(x_gained, 1)

                def out_steps(i, steps):
                    for s in steps:
                        copy_low(buf_a if s % 2 else buf_b, i * 4 + (unit_of_out(layer) + s),
                                 sum_of_out(layer) + s - 1)
                        n = unit_of_out(layer) + s + HIGH_AHEAD
                        if not isinstance(i, int) or (s < 4 and n + 4 * i < UNITS):
                            high(4, n, i)
                        if s % 2 == 0:
                            update_x(i, s // 2 - 1)

                with act.Fori(0, OUT_BLOCKS // 2 - 1) as i:
                    out_steps(i, range(1, 5))
                out_steps(OUT_BLOCKS // 2 - 1, range(1, 4 if last_layer else 5))
                if last_layer:
                    last_step()
            root(DEPTH + 1)

        @block.vector
        def _(dve):
            def low(step, at, i):
                slot = slot_of(at)
                if at >= SLOTS:
                    dve.wait_ge(units_done, i * step + (at + 1 - SLOTS))
                dve.wait_ge(hi_ready, i * step + (at + 1))
                dve.tensor_tensor(w_lo[slot][:, :, :], raw[slot][:, :, :], w_hi[slot][:, :, :].bitcast(F32),
                                  ALU.subtract).then_inc(lo_ready, 1)

            def low_x(tile, gain_at):
                for lane in range(LANES):
                    v = dve.scalar_tensor_tensor(
                        out=x_hl[:, bass.ds(tile + lane, 1), 1, :], in0=x[:, bass.ds(tile + lane, 1), :],
                        scalar=params[:, bass.ds(tile + (gain_at + lane), 1)],
                        in1=x_hl[:, bass.ds(tile + lane, 1), 0, :].bitcast(F32),
                        op0=ALU.mult, op1=ALU.subtract)
                v.then_inc(x_low, 1)

            def low_y(tile):
                return dve.tensor_tensor(y_hl[:, bass.ds(tile, 2), 1, :], buf_a[:, :, :],
                                         y_hl[:, bass.ds(tile, 2), 0, :].bitcast(F32), ALU.subtract)

            def leave_psum(dst, step, at, i):
                dve.wait_ge(low_copied, i * step + (at + 1))
                dve.tensor_tensor(dst[:, :, :], acc[at % 2][:, :, 0:SEQ], dst[:, :, :],
                                  ALU.add).then_inc(acc_free, 1)

            def factor(dst, step, at, i, rs, then_wait=True):
                dve.wait_ge(acc_free, freed(step, at, i))
                dve.tensor_tensor(dst[:, :, :], dst[:, :, :], rs, ALU.mult).then_inc(scaled, 1)
                if then_wait:
                    dve.wait_ge(scaled, i * step + (at + 1))

            dve.memset(mean_mat[:, :], 1.0 / CONV_WIDTH).then_inc(mean_set, 1)
            dve.memset(eps, EPS).then_inc(eps_set, 1)
            for r in range(2):
                dve.memset(scores[:, r, 0:CHUNK], NEG).then_inc(acc_free, 1)
            dve.memset(conv_in[:, :, 0:CONV_TAPS - 1], 0.0).then_inc(pads_set, 1)

            dve.wait_ge(params_landed, 16)
            def low_part(n, q):
                rows = part_rows(n, q)
                dve.wait_ge(*part_done(n, q, part_high, hi_ready))
                dve.tensor_tensor(w_lo[n][:, rows, :], raw[n][:, rows, :], w_hi[n][:, rows, :].bitcast(F32),
                                  ALU.subtract).then_inc(part_done(n, q, part_low, lo_ready)[0], 1)

            for t in range(TILES // 2):
                low_part(t // PARTS[0], t % PARTS[0])
                dve.wait_ge(x_high, t + 1)
                low_x(2 * t, NORM_AT)
            for n in range(2, SLOTS):
                for q in range(PARTS[n]):
                    low_part(n, q)
            dve.wait_ge(consts_landed, 16)
            dve.wait_ge(pads_set, 1)

            def factor_of_x(n):
                dve.wait_ge(x_root, n)
                dve.reciprocal(rs_x[:, :], rs_x[:, :]).then_inc(x_rs, 1)
                dve.wait_ge(x_rs, n)

            for layer in range(DEPTH):
                base, kv_sum = LAYER_UNITS * layer, LAYER_SUMS * layer
                if layer:
                    low(0, base + LOW_AHEAD, 0)
                    low(0, base + 1 + LOW_AHEAD, 0)
                dve.memset(v_pad[:, 0:CHUNK], 0.0).then_inc(v_padded, 1)
                leave_psum(buf_a, 0, kv_sum, 0)
                factor_of_x(layer + 1)
                dve.wait_ge(v_padded, layer + 1)
                dve.wait_ge(acc_free, freed(0, kv_sum, 0))
                dve.tensor_tensor(v_pad[:, CHUNK:CHUNK + SEQ], buf_a[:, 1, :], rs_x[:, :],
                                  ALU.mult).then_inc(v_scaled, 1)
                low(0, unit_of_group(layer) + LOW_AHEAD, 0)
                dve.tensor_tensor(buf_a[:, 0, :], buf_a[:, 0, :], rs_x[:, :], ALU.mult).then_inc(scaled, 1)
                dve.wait_ge(scaled, kv_sum + 1)
                dve.wait_ge(v_scaled, layer + 1)
                dve.stream_shuffle(buf_b[:, 0, :], buf_a[:, 0, :], SWAP).then_inc(k_swapped, 1)
                dve.tensor_tensor(buf_a[:, 1, :], buf_a[:, 0, :], consts[:, COS_AT:COS_AT + SEQ],
                                  ALU.mult).then_inc(k_cos, 1)
                dve.wait_ge(k_swapped, layer + 1)
                dve.tensor_tensor(buf_b[:, 1, :], buf_b[:, 0, :], consts[:, SIN_AT:SIN_AT + SEQ],
                                  ALU.mult).then_inc(k_sin, 1)
                low(0, unit_of_group(layer) + 1 + LOW_AHEAD, 0)

                def group(i, steps):
                    it = i + (layer * GROUPS + 1)
                    it2 = i * 2 + (layer * GROUPS * 2 + 1)

                    def leave(dst, j):
                        leave_psum(dst, GROUP_BLOCKS, sum_of_group(layer) + j, i)

                    def times_rs(dst, j, then_wait=True):
                        factor(dst, GROUP_BLOCKS, sum_of_group(layer) + j, i, rs_x2, then_wait)

                    for s in steps:
                        if s == 2:
                            leave(buf_c, 0)
                            times_rs(buf_c, 0)
                            dve.wait_ge(k_ready, 4 * (layer + 1))
                            cos_by_lane = cos2.rearrange("p j (c n) -> p j c n", c=CHUNKS)
                            dve.tensor_tensor(q_by_lane, by_lane(buf_c), cos_by_lane, ALU.mult).then_inc(q_cos, 1)
                            dve.stream_shuffle(buf_b[:, :, :], buf_c[:, :, :], SWAP).then_inc(q_swapped, 1)
                            dve.wait_ge(q_swapped, it)
                            dve.tensor_tensor(buf_b[:, :, :], buf_b[:, :, :], sin2, ALU.mult).then_inc(q_sin, 1)
                            dve.wait_ge(q_cos, it)
                            dve.wait_ge(q_sin, it)
                            dve.tensor_tensor(q_by_lane, q_by_lane, by_lane(buf_b), ALU.add).then_inc(q_ready, 1)
                        if s == 4:
                            leave(buf_d, 1)
                            times_rs(buf_d, 1, False)
                        if s == 6:
                            leave(buf_a, 2)
                            times_rs(buf_a, 2, False)
                        if s == 8:
                            leave(buf_b, 3)
                            times_rs(buf_b, 3)
                            dve.tensor_tensor(conv_in[:, :, CONV_TAPS - 1:], buf_a[:, :, :], buf_b[:, :, :],
                                              ALU.mult).then_inc(cu_ready, 1)
                            dve.wait_ge(cu_ready, it)
                            for tap, done in enumerate((tap0, tap1, tap2)):
                                for lane in range(LANES):
                                    src = conv_in[:, lane, tap:tap + SEQ]
                                    w = group_param(layer, i, G_TAP + tap * LANES + lane, 1)
                                    if tap == 0:
                                        dve.tensor_scalar(buf_c[:, lane, :], src, w, None,
                                                          ALU.mult).then_inc(done, 1)
                                    else:
                                        dve.wait_ge((tap0, tap1)[tap - 1], it2 + lane)
                                        dve.scalar_tensor_tensor(
                                            out=buf_c[:, lane, :], in0=src, scalar=w, in1=buf_c[:, lane, :],
                                            op0=ALU.mult, op1=ALU.add).then_inc(done, 1)
                        if s == 9:
                            dve.wait_ge(attn_copied, it)
                            for lane in range(LANES):
                                dve.scalar_tensor_tensor(
                                    out=buf_a[:, lane, :], in0=buf_b[:, lane, :],
                                    scalar=group_param(layer, i, G_ATTN + lane, 1), in1=buf_d[:, lane, :],
                                    op0=ALU.mult, op1=ALU.mult).then_inc(attn_gated, 1)
                            dve.wait_ge(attn_high, it)
                            low_y(i * 2).then_inc(attn_split, 1)
                        if s == 10:
                            leave(buf_a, 4)
                            times_rs(buf_a, 4)
                            dve.wait_ge(tap2, it2 + 1)
                            dve.tensor_tensor(buf_d[:, :, :], buf_a[:, :, :], buf_c[:, :, :],
                                              ALU.mult).then_inc(conv_ready, 1)
                        if s == 5:
                            dve.wait_ge(exp_ready, it)
                            dve.tensor_tensor(inv_den, row_sum, sink_exp, ALU.add).then_inc(den_ready, 1)
                            dve.wait_ge(den_ready, it)
                            dve.reciprocal(inv_den, inv_den).then_inc(inv_ready, 1)
                            dve.wait_ge(inv_ready, it)
                            for r in range(2):
                                by = inv_den[:, CHUNKS * r:CHUNKS * (r + 1)].unsqueeze(2).to_broadcast(
                                    [P, CHUNKS, P])
                                dve.tensor_tensor(probs[r][:, :, :], probs[r][:, :, :], by,
                                                  ALU.mult).then_inc(probs_ready, 1)
                        if s == 12:
                            leave(buf_b, 5)
                            times_rs(buf_b, 5, False)
                            dve.wait_ge(conv_squared, it)
                            dve.wait_ge(conv_gate, it)
                            for lane in range(LANES):
                                dve.scalar_tensor_tensor(
                                    out=buf_a[:, lane, :], in0=buf_d[:, lane, :],
                                    scalar=group_param(layer, i, G_CONV + lane, 1), in1=buf_b[:, lane, :],
                                    op0=ALU.mult, op1=ALU.mult).then_inc(conv_gated, 1)
                            dve.wait_ge(conv_high, it)
                            low_y(i * 2 + HALF).then_inc(conv_split, 1)
                        low(GROUP_UNITS, unit_of_group(layer) + s + LOW_AHEAD, i)
                        if s == 4:
                            dve.wait_ge(scores_ready, it)
                            sink = group_param(layer, i, G_SINK, 8)
                            for r in range(2):
                                dve.tensor_reduce(row_max[:, CHUNKS * r:CHUNKS * (r + 1)],
                                                  chunks(scores[:, r, :]), AX_X, ALU.max).then_inc(max_ready, 1)
                            dve.wait_ge(max_ready, it2 + 1)
                            dve.scalar_tensor_tensor(out=bound, in0=row_max, scalar=SCALE, in1=sink,
                                                     op0=ALU.mult, op1=ALU.max).then_inc(bounded, 1)
                            dve.wait_ge(bounded, it)
                            dve.tensor_scalar(neg_max, bound, -1.0, None, ALU.mult).then_inc(negated, 1)
                            dve.tensor_tensor(sink_exp, sink, bound, ALU.subtract).then_inc(sink_less, 1)
                with dve.Fori(0, GROUPS - 1) as i:
                    group(i, range(2, GROUP_UNITS + 2))
                group(GROUPS - 1, range(2, GROUP_UNITS + 1))

                leave_psum(buf_a, 0, sum_of_out(layer), 0)
                dve.wait_ge(roots_ready, layer + 1)
                dve.reciprocal(rs_ac[:, :, :], rs_ac[:, :, :]).then_inc(rs_ready, 1)
                dve.wait_ge(rs_ready, layer + 1)
                last_layer = layer == DEPTH - 1

                def out_steps(i, steps):
                    for s in steps:
                        at = sum_of_out(layer) + s - 1
                        dst = buf_a if s % 2 else buf_b
                        if s != 1:
                            leave_psum(dst, 4, at, i)
                        factor(dst, 4, at, i, rs_a2 if s % 2 else rs_c2, s % 2 == 0)
                        b = s // 2 - 1
                        done = i * 2 + (OUT_BLOCKS * layer + b + 1)
                        if s % 2 == 0:
                            tiles = x[:, bass.ds(i * 4 + 2 * b, 2), :]
                            dve.wait_ge(x_plus_attn, done)
                            dve.tensor_tensor(tiles, tiles, buf_b[:, :, :], ALU.add).then_inc(x_new, 1)
                        n = unit_of_out(layer) + s + LOW_AHEAD
                        if not isinstance(i, int) or (s < 4 and n + 4 * i < UNITS):
                            low(4, n, i)
                        if s % 2 == 0 and not last_layer:
                            dve.wait_ge(x_new, done)
                            dve.wait_ge(x_high, done + OUT_BLOCKS)
                            low_x(i * 4 + 2 * b, NORM_AT + TILES * (layer + 1))
                        if s == 4 and not isinstance(i, int):
                            leave_psum(buf_a, 4, at + 1, i)

                with dve.Fori(0, OUT_BLOCKS // 2 - 1) as i:
                    out_steps(i, range(1, 5))
                out_steps(OUT_BLOCKS // 2 - 1, range(1, 4 if last_layer else 5))
            last_sum = DEPTH * LAYER_SUMS - 1
            for lane in range(LANES):
                dst, tile = buf_b[:, lane, :], x[:, TILES - LANES + lane, :]
                dve.wait_ge(low_copied, last_sum + lane + 1)
                dve.tensor_tensor(dst, acc[last_sum % 2][:, lane, 0:SEQ], dst, ALU.add).then_inc(acc_free, 1)
                dve.wait_ge(acc_free, freed(0, last_sum, 0) + lane)
                dve.tensor_tensor(dst, dst, rs_ac[:, 1, :], ALU.mult).then_inc(scaled, 1)
                dve.wait_ge(scaled, last_sum + lane + 1)
                dve.wait_ge(x_plus_attn, OUT_BLOCKS * DEPTH)
                dve.tensor_tensor(tile, tile, dst, ALU.add).then_inc(x_new, 1)
            factor_of_x(DEPTH + 1)
            for b in range(OUT_BLOCKS):
                dve.wait_ge(x_gained, b + 1)
                dve.tensor_tensor(x[:, 2 * b:2 * b + 2, :], x[:, 2 * b:2 * b + 2, :], rs_x2,
                                  ALU.mult).then_inc(x_final, 1)

        @block.gpsimd
        def _(pool):
            def add_square(src, sums, squared, squares, summed, adds):
                pool.tensor_tensor(square[:, :, :], src, src, ALU.mult).then_inc(squared, 1)
                pool.wait_ge(squared, squares)
                pool.tensor_tensor(sums[:, :, :], sums[:, :, :], square[:, :, :], ALU.add).then_inc(summed, 1)
                pool.wait_ge(summed, adds)

            def fold(sums, folded):
                pool.tensor_tensor(sums[:, 0, :], sums[:, 0, :], sums[:, 1, :], ALU.add).then_inc(folded, 1)

            zeroed = 0
            pool.memset(sum_ax[:, :, :], 0.0).then_inc(sums_zeroed, 1)
            zeroed += 1
            pool.wait_ge(sums_zeroed, zeroed)
            for t in range(EARLY_SQUARES[0]):
                pool.wait_ge(x_landed[t], 16)
                add_square(x[:, 2 * t:2 * t + 2, :], sum_ax, x_squared, t + 1, x_summed, t + 1)
            for n, src in enumerate((buf_b, buf_d)):
                pool.wait_ge(early_squared, n + 1)
                pool.tensor_tensor(sum_ax[:, :, :], sum_ax[:, :, :], src[:, :, :], ALU.add).then_inc(x_summed, 1)
                pool.wait_ge(x_summed, EARLY_SQUARES[n] + 1)

            for layer in range(DEPTH):
                fold(sum_ax, x_folded)
                pool.wait_ge(x_mean, layer + 1)
                pool.memset(sum_ax[:, :, :], 0.0).then_inc(sums_zeroed, 1)
                pool.memset(sum_c[:, :, :], 0.0).then_inc(sums_zeroed, 1)
                zeroed += 2
                pool.wait_ge(sums_zeroed, zeroed)
                pool.wait_ge(k_cos, layer + 1)
                pool.wait_ge(k_sin, layer + 1)
                for j in range(LANES):
                    src = slice(j * HEAD, (j + 1) * HEAD)
                    for r in range(2):
                        pool.tensor_tensor(k_dup[r * HEAD:(r + 1) * HEAD, j, :], buf_a[src, 1, :],
                                           buf_b[src, 1, :], ALU.add).then_inc(k_ready, 1)
                with pool.Fori(0, GROUPS) as i:
                    it = i + (layer * GROUPS + 1)
                    pool.wait_ge(attn_copied, it)
                    add_square(buf_b[:, :, :], sum_ax, attn_squared, it, attn_summed, it)
                    pool.wait_ge(conv_ready, it)
                    add_square(buf_d[:, :, :], sum_c, conv_squared, it, conv_summed, it)
                fold(sum_ax, groups_folded)
                fold(sum_c, groups_folded)
                pool.wait_ge(means_ready, layer + 1)
                pool.memset(sum_ax[:, :, :], 0.0).then_inc(sums_zeroed, 1)
                zeroed += 1
                pool.wait_ge(sums_zeroed, zeroed)

                def add_attn(i):
                    pool.wait_ge(scaled, i * 2 + (sum_of_out(layer) + 1))
                    tiles = x[:, bass.ds(i * 2, 2), :]
                    pool.tensor_tensor(tiles, tiles, buf_a[:, :, :], ALU.add).then_inc(x_plus_attn, 1)

                def out_block(i):
                    add_attn(i)
                    pool.wait_ge(x_new, i + (OUT_BLOCKS * layer + 1))
                    block_of_x = x[:, :, :].rearrange("p (b j) n -> p b (j n)", j=LANES)
                    add_square(block_of_x[:, bass.ds(i, 1), :], sum_ax,
                               x_squared, i + (EARLY_SQUARES[0] + OUT_BLOCKS * layer + 1),
                               x_summed, i + (OUT_BLOCKS * (layer + 1) + 1))

                with pool.Fori(0, OUT_BLOCKS - 1) as i:
                    out_block(i)
                if layer < DEPTH - 1:
                    out_block(OUT_BLOCKS - 1)
                else:
                    fold(sum_ax, x_folded)
                    add_attn(OUT_BLOCKS - 1)


def kernel(x, norm_g, w_in, conv_w, sinks, gn_conv, gn_attn, w_out, final_g):
    import numpy as np
    import concourse.bacc as bacc
    from concourse.bass_utils import run_bass_kernel_spmd

    x, norm_g, w_in, conv_w, sinks, gn_conv, gn_attn, w_out, final_g = (
        np.asarray(a) for a in (x, norm_g, w_in, conv_w, sinks, gn_conv, gn_attn, w_out, final_g))

    b_at, c_at, u_at, z_at, q_at = (n * CONV_WIDTH for n in range(5))
    k_at = q_at + ATTN_WIDTH
    za_at = k_at + 2 * P
    blocks = [(k_at, k_at + P)]
    for i in range(GROUPS):
        lanes = [2 * i * P, (2 * i + 1) * P]
        for start in (q_at, za_at, c_at, u_at, b_at, z_at):
            blocks.append(tuple(start + n for n in lanes))
    attn_rows = [CONV_WIDTH + t * P for t in range(HALF)]
    conv_rows = [t * P for t in range(HALF)]
    weights = np.empty((UNITS, P, HALF, BLOCK), w_in.dtype)
    n = 0
    for layer in range(DEPTH):
        w = w_in[layer].reshape(2, HALF, P, -1)
        for lanes in blocks:
            for half in range(2):
                for lane, at in enumerate(lanes):
                    weights[n, :, :, lane * P:(lane + 1) * P] = w[half, :, :, at:at + P].transpose(1, 0, 2)
                n += 1
        for b in range(OUT_BLOCKS):
            for rows in (attn_rows, conv_rows):
                for k, r in enumerate(rows):
                    weights[n, :, k, :] = w_out[layer, r:r + P, b * BLOCK:(b + 1) * BLOCK]
                n += 1

    def by_tile(a):
        return a.reshape(-1, P).T

    params = np.empty((P, PARAMS), x.dtype)
    for layer in range(DEPTH):
        for i in range(GROUPS):
            at = (layer * GROUPS + i) * GROUP_COLS
            for lane in range(LANES):
                tile = 2 * i + lane
                for tap in range(CONV_TAPS):
                    params[:, at + G_TAP + tap * LANES + lane] = by_tile(conv_w[layer, tap])[:, tile]
                params[:, at + G_CONV + lane] = by_tile(gn_conv[layer])[:, tile]
                params[:, at + G_ATTN + lane] = by_tile(gn_attn[layer])[:, tile]
                for r in range(2):
                    params[lane * CHUNK:(lane + 1) * CHUNK,
                           at + G_SINK + r * CHUNKS:at + G_SINK + (r + 1) * CHUNKS] = sinks[layer, 2 * tile + r]
        params[:, NORM_AT + layer * TILES:NORM_AT + (layer + 1) * TILES] = by_tile(norm_g[layer])
    params[:, FINAL_AT:FINAL_AT + TILES] = by_tile(final_g)

    half = HEAD // 8
    inv_freq = np.float32(500000.0) ** (-np.arange(half, dtype=np.float32) * np.float32(2.0)
                                        / np.float32(2 * half))
    angle = np.arange(SEQ, dtype=np.float32)[:, None] * inv_freq[None, :].astype(np.float32)
    consts = np.zeros((P, CONSTS), np.float32)
    consts[:, COS_AT:COS_AT + SEQ] = 1.0
    for p in range(P):
        d = p % HEAD
        if d < 2 * half:
            consts[p, COS_AT:COS_AT + SEQ] = np.cos(angle[:, d % half])
            consts[p, SIN_AT:SIN_AT + SEQ] = np.sin(angle[:, d % half]) * (-1.0 if d < half else 1.0)
    consts[:, IDENT_AT:IDENT_AT + P] = np.eye(P, dtype=np.float32)

    arrays = {
        "x_t": np.ascontiguousarray(x[0].T.reshape(TILES, P, SEQ).transpose(1, 0, 2)),
        "weights": weights,
        "params": params,
        "consts": consts,
    }
    nc = bacc.Bacc("TRN2", target_bir_lowering=False, num_devices=1)
    args = [nc.dram_tensor("in_" + name, a.shape, mybir.dt.from_np(a.dtype), kind="ExternalInput").ap()
            for name, a in arrays.items()]
    out = nc.dram_tensor("out_t", (P, TILES, SEQ), F32, kind="ExternalOutput").ap()
    build(nc, *args, out)
    inputs = {"in_" + name: a for name, a in arrays.items()}
    got = run_bass_kernel_spmd(nc, [inputs], core_ids=[0]).results[0]["out_t"]
    return np.ascontiguousarray(got.transpose(1, 0, 2).reshape(D_MODEL, SEQ).T)[None]
```
